# Optimizing a Trainium2 kernel written in Bass

```python
import jax, jax.numpy as jnp
from jax import lax
import numpy as np

D_MODEL = 1024
BATCH = 1
SEQ = 128
DEPTH = 2
DEC_BATCH = 1
DEC_SEQ = 512
PAST_LEN = 128

GRID_W = 64
N_MIXERS = 2
N_MLA_LAYERS = (DEPTH + 1) // 2
N_NAT_LAYERS = DEPTH // 2
MLA_HEADS = 16
MLA_NOPE_DIM = 64
MLA_ROPE_DIM = 32
MLA_V_DIM = 64
MLA_Q_LORA = 384
MLA_KV_LORA = 256
MLA_IN_DIM = MLA_Q_LORA + MLA_KV_LORA + MLA_ROPE_DIM
MLA_SCALE = (MLA_NOPE_DIM + MLA_ROPE_DIM) ** -0.5
ROPE_THETA = 10000.0
NAT_HEADS = 16
NAT_HEAD_DIM = D_MODEL // NAT_HEADS
NAT_SCALE = NAT_HEAD_DIM ** -0.5
WIN_H = 8
WIN_W = 16
Q_COLS = WIN_W
K_COLS = 2 * WIN_W
N_COL_BLOCKS = GRID_W // Q_COLS
N_EXPERTS = 16
N_GROUPS = 4
EXPERTS_PER_GROUP = N_EXPERTS // N_GROUPS
TOPK_GROUPS = 1
TOP_K = 2
D_EXPERT = 256
Q_BLOCK = 128
NORM_EPS = 1e-6
NEG_INF = -1e30

kernel_name = 'hybrid_mla_natten_grouped_moe_diffusion_step'

def rmsnorm(x, g):
    xf = x.astype(jnp.float32)
    xf = xf * lax.rsqrt(jnp.mean(xf * xf, axis=-1, keepdims=True) + NORM_EPS)
    return (xf * g.astype(jnp.float32)).astype(x.dtype)

def ada_modulation(cond, w, b):
    mod = jax.nn.silu(cond) @ w + b
    return [m[:, None, :] for m in jnp.split(mod, 6, axis=-1)]

def modulate(h, shift, scale):
    return h * (1.0 + scale) + shift

def axial_rope_angles(n_tokens):
    t = jnp.arange(n_tokens)
    row = (t // GRID_W).astype(jnp.float32)
    col = (t % GRID_W).astype(jnp.float32)
    n_freq = MLA_ROPE_DIM // 4
    inv_freq = ROPE_THETA ** (-jnp.arange(n_freq, dtype=jnp.float32) / n_freq)
    return row[:, None] * inv_freq, col[:, None] * inv_freq

def rotate_pairs(x, ang):
    x1, x2 = jnp.split(x, 2, axis=-1)
    cos = jnp.cos(ang).astype(x.dtype)
    sin = jnp.sin(ang).astype(x.dtype)
    return jnp.concatenate([x1 * cos - x2 * sin, x1 * sin + x2 * cos], axis=-1)

def apply_axial_rope(x, ang_row, ang_col):
    half = MLA_ROPE_DIM // 2
    return jnp.concatenate([rotate_pairs(x[..., :half], ang_row),
                            rotate_pairs(x[..., half:], ang_col)], axis=-1)

def blocked_attention(q, k, v, scale):
    B, S, H, Dk = q.shape
    nb = S // Q_BLOCK
    qb = jnp.moveaxis(q.reshape(B, nb, Q_BLOCK, H, Dk), 1, 0)

    def one_block(q_blk):
        s = jnp.einsum('bqhd,bkhd->bhqk', q_blk, k).astype(jnp.float32) * scale
        p = jax.nn.softmax(s, axis=-1).astype(v.dtype)
        return jnp.einsum('bhqk,bkhd->bqhd', p, v)

    out = lax.map(one_block, qb)
    return jnp.moveaxis(out, 0, 1).reshape(B, S, H, v.shape[-1])

def mla_compress(h, w_in, q_norm, w_uq, kv_norm):
    B, S, _ = h.shape
    lat = h @ w_in
    c_q = lat[..., :MLA_Q_LORA]
    c_kv = lat[..., MLA_Q_LORA:MLA_Q_LORA + MLA_KV_LORA]
    k_rope = lat[..., MLA_Q_LORA + MLA_KV_LORA:]
    q = (rmsnorm(c_q, q_norm) @ w_uq).reshape(B, S, MLA_HEADS, MLA_NOPE_DIM + MLA_ROPE_DIM)
    return q, rmsnorm(c_kv, kv_norm), k_rope

def mla_attend(q, c_kv, k_rope, w_ukv, w_o):
    B, S = q.shape[0], q.shape[1]
    T = c_kv.shape[1]
    kv = (c_kv @ w_ukv).reshape(B, T, MLA_HEADS, MLA_NOPE_DIM + MLA_V_DIM)
    k_nope, v = kv[..., :MLA_NOPE_DIM], kv[..., MLA_NOPE_DIM:]
    k = jnp.concatenate([k_nope, jnp.broadcast_to(k_rope[:, :, None, :], (B, T, MLA_HEADS, MLA_ROPE_DIM))], axis=-1)
    o = blocked_attention(q, k, v, MLA_SCALE)
    return o.reshape(B, S, MLA_HEADS * MLA_V_DIM) @ w_o

def nat_qkv(h, w_qkv):
    B, S, _ = h.shape
    q, k, v = jnp.split(h @ w_qkv, 3, axis=-1)
    shp = (B, S, NAT_HEADS, NAT_HEAD_DIM)
    return q.reshape(shp), k.reshape(shp), v.reshape(shp)

def neighbourhood_attention(q, k, v, k_ctx, v_ctx, rpb):
    B, S, H, Dh = q.shape
    rows = S // GRID_W
    kh = min(WIN_H, rows)
    r = np.arange(rows)
    row_idx = np.clip(r - kh // 2, 0, rows - kh)[:, None] + np.arange(kh)
    cb = np.arange(N_COL_BLOCKS)
    col_idx = np.clip(cb * Q_COLS - WIN_W // 2, 0, GRID_W - K_COLS)[:, None] + np.arange(K_COLS)
    q_col = cb[:, None] * Q_COLS + np.arange(Q_COLS)
    q_cs = np.clip(q_col - WIN_W // 2, 0, GRID_W - WIN_W)
    valid = (col_idx[:, None, :] >= q_cs[:, :, None]) & (col_idx[:, None, :] < q_cs[:, :, None] + WIN_W)
    d_row = row_idx - r[:, None] + (WIN_H - 1)
    d_col = np.clip(col_idx[:, None, :] - q_col[:, :, None] + (WIN_W - 1), 0, 2 * WIN_W - 2)
    bias = rpb.astype(jnp.float32)[:, d_row[:, None, None, :, None], d_col[None, :, :, None, :]]
    bias = jnp.where(valid[None, None, :, :, None, :], bias, NEG_INF)
    bias = bias.reshape(H, rows, N_COL_BLOCKS, Q_COLS, kh * K_COLS)

    qg = q.reshape(B, rows, N_COL_BLOCKS, Q_COLS, H, Dh)
    kg = k.reshape(B, rows, GRID_W, H, Dh)[:, row_idx][:, :, :, col_idx]
    vg = v.reshape(B, rows, GRID_W, H, Dh)[:, row_idx][:, :, :, col_idx]
    s_loc = jnp.einsum('brnqhd,brankhd->bhrnqak', qg, kg).astype(jnp.float32)
    s_loc = s_loc.reshape(B, H, rows, N_COL_BLOCKS, Q_COLS, kh * K_COLS) * NAT_SCALE + bias
    s_ctx = jnp.einsum('brnqhd,bchd->bhrnqc', qg, k_ctx).astype(jnp.float32) * NAT_SCALE
    p = jax.nn.softmax(jnp.concatenate([s_loc, s_ctx], axis=-1), axis=-1).astype(v.dtype)
    n_loc = kh * K_COLS
    p_loc = p[..., :n_loc].reshape(B, H, rows, N_COL_BLOCKS, Q_COLS, kh, K_COLS)
    p_ctx = p[..., n_loc:]
    o = (jnp.einsum('bhrnqak,brankhd->brnqhd', p_loc, vg)
         + jnp.einsum('bhrnqc,bchd->brnqhd', p_ctx, v_ctx))
    return o.reshape(B, S, H * Dh)

def grouped_moe(h, w_router, router_bias, w_gate, w_up, w_down):
    shp = h.shape
    t = h.reshape(-1, shp[-1])
    T = t.shape[0]
    scores = jax.nn.sigmoid((t @ w_router).astype(jnp.float32))
    biased = scores + router_bias.astype(jnp.float32)
    grp = biased.reshape(T, N_GROUPS, EXPERTS_PER_GROUP)
    group_score = jnp.sum(lax.top_k(grp, 2)[0], axis=-1)
    _, top_group = lax.top_k(group_score, TOPK_GROUPS)
    group_mask = jnp.sum(jax.nn.one_hot(top_group, N_GROUPS, dtype=jnp.float32), axis=1)
    expert_mask = jnp.repeat(group_mask, EXPERTS_PER_GROUP, axis=-1) > 0
    _, top_e = lax.top_k(jnp.where(expert_mask, biased, NEG_INF), TOP_K)
    w_sel = jnp.take_along_axis(scores, top_e, axis=-1)
    w_sel = w_sel / jnp.sum(w_sel, axis=-1, keepdims=True)
    gates = jnp.sum(jax.nn.one_hot(top_e, N_EXPERTS, dtype=jnp.float32) * w_sel[..., None], axis=1)
    act = jax.nn.silu(jnp.einsum('td,edf->tef', t, w_gate)) * jnp.einsum('td,edf->tef', t, w_up)
    act = act * gates.astype(act.dtype)[..., None]
    return jnp.einsum('tef,efd->td', act, w_down).reshape(shp)

def setup_inputs(seed: int = 0) -> dict:
    key = jax.random.key(seed)
    ks = jax.random.split(key, 27)
    nrm = jax.random.normal
    f32 = jnp.float32
    D = D_MODEL
    return {
        'x_prompt': nrm(ks[0], (BATCH, SEQ, D), f32),
        'x_sample': nrm(ks[1], (DEC_BATCH, DEC_SEQ, D), f32),
        'cache_mla_ckv': nrm(ks[2], (DEC_BATCH, N_MLA_LAYERS, PAST_LEN, MLA_KV_LORA), f32),
        'cache_mla_krope': nrm(ks[3], (DEC_BATCH, N_MLA_LAYERS, PAST_LEN, MLA_ROPE_DIM), f32),
        'cache_nat_k': nrm(ks[4], (DEC_BATCH, N_NAT_LAYERS, PAST_LEN, NAT_HEADS, NAT_HEAD_DIM), f32),
        'cache_nat_v': nrm(ks[5], (DEC_BATCH, N_NAT_LAYERS, PAST_LEN, NAT_HEADS, NAT_HEAD_DIM), f32),
        'c': nrm(ks[6], (DEC_BATCH, D), f32),
        'c_ctx': nrm(ks[7], (D,), f32),
        'w_ada': nrm(ks[8], (DEPTH, D, 6 * D), f32) * (0.5 * D ** -0.5),
        'b_ada': nrm(ks[9], (DEPTH, 6 * D), f32) * 0.02,
        'norm_mix': 1.0 + 0.02 * nrm(ks[10], (DEPTH, D), f32),
        'norm_ffn': 1.0 + 0.02 * nrm(ks[11], (DEPTH, D), f32),
        'norm_final': 1.0 + 0.02 * nrm(ks[12], (D,), f32),
        'mla_w_in': nrm(ks[13], (N_MLA_LAYERS, D, MLA_IN_DIM), f32) * D ** -0.5,
        'mla_q_norm': 1.0 + 0.02 * nrm(ks[14], (N_MLA_LAYERS, MLA_Q_LORA), f32),
        'mla_w_uq': nrm(ks[15], (N_MLA_LAYERS, MLA_Q_LORA, MLA_HEADS * (MLA_NOPE_DIM + MLA_ROPE_DIM)), f32) * MLA_Q_LORA ** -0.5,
        'mla_kv_norm': 1.0 + 0.02 * nrm(ks[16], (N_MLA_LAYERS, MLA_KV_LORA), f32),
        'mla_w_ukv': nrm(ks[17], (N_MLA_LAYERS, MLA_KV_LORA, MLA_HEADS * (MLA_NOPE_DIM + MLA_V_DIM)), f32) * MLA_KV_LORA ** -0.5,
        'mla_w_o': nrm(ks[18], (N_MLA_LAYERS, MLA_HEADS * MLA_V_DIM, D), f32) * (MLA_HEADS * MLA_V_DIM) ** -0.5,
        'nat_w_qkv': nrm(ks[19], (N_NAT_LAYERS, D, 3 * D), f32) * D ** -0.5,
        'nat_rpb': nrm(ks[20], (N_NAT_LAYERS, NAT_HEADS, 2 * WIN_H - 1, 2 * WIN_W - 1), f32) * 0.1,
        'nat_w_o': nrm(ks[21], (N_NAT_LAYERS, D, D), f32) * D ** -0.5,
        'w_router': nrm(ks[22], (D, N_EXPERTS), f32) * D ** -0.5,
        'router_bias': nrm(ks[23], (N_EXPERTS,), f32) * 0.01,
        'moe_w_gate': nrm(ks[24], (DEPTH, N_EXPERTS, D, D_EXPERT), f32) * D ** -0.5,
        'moe_w_up': nrm(ks[25], (DEPTH, N_EXPERTS, D, D_EXPERT), f32) * D ** -0.5,
        'moe_w_down': nrm(ks[26], (DEPTH, N_EXPERTS, D_EXPERT, D), f32) * D_EXPERT ** -0.5,
    }

def reference(x_prompt, x_sample, cache_mla_ckv, cache_mla_krope, cache_nat_k, cache_nat_v,
              c, c_ctx, w_ada, b_ada, norm_mix, norm_ffn, norm_final,
              mla_w_in, mla_q_norm, mla_w_uq, mla_kv_norm, mla_w_ukv, mla_w_o,
              nat_w_qkv, nat_rpb, nat_w_o, w_router, router_bias,
              moe_w_gate, moe_w_up, moe_w_down):
    B, S, D = x_prompt.shape
    n_lat = x_sample.shape[1]
    ang_row, ang_col = axial_rope_angles(n_lat)
    xc, xs = x_prompt, x_sample
    new_ckv, new_krope, new_k, new_v = [], [], [], []
    for layer in range(DEPTH):
        sh_a_c, sc_a_c, g_a_c, sh_f_c, sc_f_c, g_f_c = ada_modulation(c_ctx[None, :], w_ada[layer], b_ada[layer])
        sh_a_s, sc_a_s, g_a_s, sh_f_s, sc_f_s, g_f_s = ada_modulation(c, w_ada[layer], b_ada[layer])
        hc = modulate(rmsnorm(xc, norm_mix[layer]), sh_a_c, sc_a_c)
        hs = modulate(rmsnorm(xs, norm_mix[layer]), sh_a_s, sc_a_s)
        j = layer // N_MIXERS
        if layer % N_MIXERS == 0:
            q_c, ckv_c, kr_c = mla_compress(hc, mla_w_in[j], mla_q_norm[j], mla_w_uq[j], mla_kv_norm[j])
            out_c = mla_attend(q_c, ckv_c, kr_c, mla_w_ukv[j], mla_w_o[j])
            new_ckv.append(ckv_c)
            new_krope.append(kr_c)
            q_s, ckv_s, kr_s = mla_compress(hs, mla_w_in[j], mla_q_norm[j], mla_w_uq[j], mla_kv_norm[j])
            q_s = jnp.concatenate([q_s[..., :MLA_NOPE_DIM],
                                   apply_axial_rope(q_s[..., MLA_NOPE_DIM:], ang_row[:, None, :], ang_col[:, None, :])], axis=-1)
            kr_s = apply_axial_rope(kr_s, ang_row, ang_col)
            out_s = mla_attend(q_s,
                               jnp.concatenate([ckv_s, cache_mla_ckv[:, j]], axis=1),
                               jnp.concatenate([kr_s, cache_mla_krope[:, j]], axis=1),
                               mla_w_ukv[j], mla_w_o[j])
        else:
            q_c, k_c, v_c = nat_qkv(hc, nat_w_qkv[j])
            out_c = blocked_attention(q_c, k_c, v_c, NAT_SCALE).reshape(B, S, D) @ nat_w_o[j]
            new_k.append(k_c)
            new_v.append(v_c)
            q_s, k_s, v_s = nat_qkv(hs, nat_w_qkv[j])
            out_s = neighbourhood_attention(q_s, k_s, v_s, cache_nat_k[:, j], cache_nat_v[:, j], nat_rpb[j]) @ nat_w_o[j]
        xc = xc + g_a_c * out_c
        xs = xs + g_a_s * out_s
        hc = modulate(rmsnorm(xc, norm_ffn[layer]), sh_f_c, sc_f_c)
        hs = modulate(rmsnorm(xs, norm_ffn[layer]), sh_f_s, sc_f_s)
        xc = xc + g_f_c * grouped_moe(hc, w_router, router_bias, moe_w_gate[layer], moe_w_up[layer], moe_w_down[layer])
        xs = xs + g_f_s * grouped_moe(hs, w_router, router_bias, moe_w_gate[layer], moe_w_up[layer], moe_w_down[layer])
    y_prompt = rmsnorm(xc, norm_final)
    y_sample = rmsnorm(xs, norm_final)
    return (y_prompt, y_sample, jnp.stack(new_ckv, axis=1), jnp.stack(new_krope, axis=1),
            jnp.stack(new_k, axis=1), jnp.stack(new_v, axis=1))


_drawn_inputs = setup_inputs


def setup_inputs(seed=0):
    import zlib

    import numpy as np

    out = dict(_drawn_inputs(seed))
    spreads = {}
    factors = {'cache_mla_krope': 3.547,
     'norm_mix': 2.925,
     'norm_final': 8.266,
     'mla_q_norm': 6.083,
     'mla_kv_norm': 2.739,
     'nat_rpb': 6.993,
     'cache_nat_k': 8.0,
     'cache_nat_v': 8.0}
    for name, (base, spread) in spreads.items():
        noise = np.random.default_rng([zlib.crc32(name.encode()), seed]).standard_normal(out[name].shape)
        drawn = base * np.exp(spread * noise) if base else spread * noise
        out[name] = __import__('jax').numpy.asarray(drawn.astype(out[name].dtype))
    for name, factor in factors.items():
        out[name] = (out[name] * factor).astype(out[name].dtype)
    return out
```

```python
from contextlib import ExitStack

import numpy as np

import concourse.bass as bass
from concourse import mybir

F32 = mybir.dt.float32
I32 = mybir.dt.int32
U32 = mybir.dt.uint32
ALU = mybir.AluOpType
ACT = mybir.ActivationFunctionType
AXX = mybir.AxisListType.X

P = 128
D = 1024
KD = D // P
NT = 5
CTX = 4
TOK = NT * P
DEPTH = 2
GRID_W, ROWS = 64, 8
H = 16
NOPE, ROPE, VD = 64, 32, 64
QD = NOPE + ROPE
QL, KVL = 384, 256
IN_DIM = QL + KVL + ROPE
MLA_SCALE = float(QD) ** -0.5
NAT_SCALE = 64.0 ** -0.5
E, G4, DE = 16, 4, 256
EPS = 1e-6
NEG = -1e30
LOCAL = 256
KEY0 = [0, 64, 192, 256]
VARIANT = [0, 1, 1, 2]
TOEP = 63
TSTART = [31, 23, 15]
TLEN = (TOEP - 15) * 8
XTILES = 9
MAXT = E + XTILES
SLOTS = (MAXT + 1) * P

C_ID, C_TRI, C_ONE = 0, 128, 256
C_MASK = 384
C_COS, C_SIN = 896, 960
C_TOK = 1024
C_I16 = 1032
C_E128 = 1048
C_X9 = 1064
C_EPS = 1073
C_EVEN = 1074
NCONST = 1078


def constants():
    c = np.zeros((P, NCONST), np.float32)
    p = np.arange(P)
    c[:, C_ID:C_ID + P] = np.eye(P)
    c[:, C_TRI:C_TRI + P] = p[:, None] < p[None, :]
    c[:, C_ONE:C_ONE + P] = 1.0
    qc, kc = p // ROWS, np.arange(LOCAL) // ROWS
    for n, (q0, k0) in enumerate(((0, 0), (48, 32))):
        q, k = q0 + qc[:, None], k0 + kc[None, :]
        start = np.clip(q - 8, 0, GRID_W - 16)
        c[:, C_MASK + n * LOCAL:C_MASK + (n + 1) * LOCAL] = np.where((k >= start) & (k < start + 16), 0.0, NEG)
    inv = (10000.0 ** (-np.arange(8, dtype=np.float32) / 8)).astype(np.float32)
    for t in range(4):
        n = t * P + p
        ang = np.stack([(n % ROWS)[:, None] * inv, (n // ROWS)[:, None] * inv], 1).astype(np.float32)
        c[:, C_COS + 16 * t:C_COS + 16 * t + 16] = np.cos(ang).reshape(P, 16)
        c[:, C_SIN + 16 * t:C_SIN + 16 * t + 16] = np.sin(ang).reshape(P, 16)
    c[:, C_TOK:C_TOK + NT] = np.arange(NT)[None, :] * P + p[:, None]
    c[:, C_I16:C_I16 + E] = np.arange(E)
    c[:, C_E128:C_E128 + E] = np.arange(E) * P
    c[:, C_X9:C_X9 + XTILES] = np.arange(XTILES)
    c[:, C_EPS] = EPS
    c[:, C_EVEN:C_EVEN + 4] = [2, 4, 6, 8]
    return c


def build(nc, a, o):
    with ExitStack() as ctx:
        def sem(name):
            return ctx.enter_context(nc.semaphore(name))

        def sb(name, n, parts=P, dt=F32):
            return ctx.enter_context(nc.sbuf_tensor(name, [parts, n], dt))

        const = sb("const", NCONST)
        X = sb("resid", NT * D)
        W = sb("weights", 3 * 4096)
        HT = sb("ht", KD * TOK)
        R = sb("rows", 6 * D)
        BIG = sb("big", 20480)
        modT = sb("modT", DEPTH * 96)
        vecT = sb("vecT", 144)
        condT = sb("condT", 16)
        modR = sb("modR", P, 96)
        latG = sb("latG", QL + KVL)
        st = sb("stats", 160)
        rt = sb("route", 1340)
        rti = sb("slot_of", 2 * NT, P, U32)
        rtx = sb("tiles", 32, 1, I32)
        wrt = sb("wrouter", KD * E)
        info = sb("info", 4)
        PS = ctx.enter_context(nc.psum_tensor("PS", [P, 8 * 512], F32))

        ident = const[:, C_ID:C_ID + P]
        ones = const[:, C_ONE:C_ONE + P]
        tri = const[:, C_TRI:C_TRI + P]

        def x_(t):
            return X[:, t * D:(t + 1) * D]

        def row(i):
            return R[:, i * D:(i + 1) * D]

        def w_(slot, k, n):
            return W[:, slot * 4096:slot * 4096 + k * n].rearrange("p (k n) -> p k n", k=k)

        def big(off, n, k=None):
            assert off + n <= 20480
            v = BIG[:, off:off + n]
            return v if k is None else v.rearrange("p (k n) -> p k n", k=k)

        def bank(b, n=512, at=0):
            return PS[:, b * 512 + at:b * 512 + at + n]

        hT = HT[:, :].rearrange("p (k t) -> p k t", k=KD)
        O = HT[:, :].rearrange("p (t n) -> p t n", t=NT)
        OT = big(0, 5120, KD)
        HB = [big(7680 + i * D, D) for i in range(3)]
        tmpw = [big(13824 + i * 512, 512) for i in range(2)]
        lat = big(0, NT * IN_DIM, NT)
        q = big(0, 7680, NT)
        kn = big(7680, 6144, 6)
        mv = big(13824, 6144, 6)
        krw = big(19968, 192, 6)
        cqT = R[:, 0:1920].rearrange("p (k t) -> p k t", k=3)
        ckvT = R[:, 1920:3456].rearrange("p (k t) -> p k t", k=2)
        qTh = [R[:, i * 640:(i + 1) * 640] for i in range(2)]
        Pm = [R[:, 1280 + i * 640:1280 + (i + 1) * 640] for i in range(2)]
        PTm = [R[:, 2560 + i * 640:2560 + (i + 1) * 640] for i in range(2)]
        kTh = [R[:, 3840 + i * 768:3840 + (i + 1) * 768] for i in range(2)]
        ckc = R[:, 5376:5632]
        ropet = rt[:, 0:1024].rearrange("p (n h x i) -> p n h x i", n=4, h=H, x=2)
        qT = big(0, 5120, KD)
        kT = big(5120, 5120, KD)
        nv = big(10240, 5120, NT)
        nvs = big(15360, 3072, 3)
        kcr = big(15360, 1024)
        kout = big(16384, 1024)
        nvc = big(18432, 1024)
        kcT = big(19456, 1024, KD)
        biasb = [R[:, i * 1152:(i + 1) * 1152].rearrange("p (v k) -> p v k", v=3) for i in range(2)]
        Pn = [R[:, 2304 + i * 384:2304 + (i + 1) * 384] for i in range(2)]
        PTn = [R[:, 3072 + i * 384:3072 + (i + 1) * 384] for i in range(2)]
        gat = big(10752, D)
        gatT = big(11776, D, KD)
        sig = big(12800, DE)
        actv = big(13056, DE)
        actT = big(13312, DE, 2)
        yb = [big(13568 + i * D, D) for i in range(2)]
        cy = [[big(15616 + (2 * i + c) * D, D) for c in range(2)] for i in range(2)]
        vecs = big(7000, 256)
        toep = BIG[0:H, 11100:11100 + 2 * ROWS * TOEP * ROWS].rearrange("h (v r d a) -> h v r d a", v=2, r=ROWS, a=ROWS)
        rpbs = BIG[0:H, 19200:19200 + 31 * 15].rearrange("h (d r) -> h d r", r=15)
        zero = big(3400, D)

        modD = nc.dram_tensor("modrows", [DEPTH * 96, P], F32).ap()
        toepD = nc.dram_tensor("toeplitz", [16, H, 2 * ROWS, TLEN], F32).ap()
        hD = [nc.dram_tensor(f"hrows{l}", [TOK, D], F32).ap() for l in range(DEPTH)]
        slotD = [nc.dram_tensor(f"slots{l}", [SLOTS, 2], F32).ap() for l in range(DEPTH)]
        yD = nc.dram_tensor("yrows", [MAXT * P, D], F32).ap()

        s_const, s_x, s_vec, s_par, s_ck = (sem(n) for n in ("const_in", "x_in", "vec_in", "gains_and_router_in", "mlacache_in"))
        s_zero, s_yz, s_toep, s_toepd, s_rpb = (sem(n) for n in (
            "zeroed", "scratch_zeroed", "toep_built", "toep_stored", "rpb_in"))
        s_vt, s_vc, s_cond, s_sg = (sem(n) for n in ("vec_transposed", "vec_copied", "cond_ready", "cond_sigmoid"))
        s_dve, s_pool, s_act = sem("dve_chain"), sem("pool_chain"), sem("act_chain")
        NORMS = ("m0", "f0", "m1", "f1", "fin")
        n_sd, n_rs, n_xn, n_ha, n_h, n_tr, n_ta, n_td = (sem(f"norm_{n}") for n in (
            "sqrt", "rstd", "xn", "scaled", "h", "transposed", "hT_act", "hT_dve"))
        n_st = [sem(f"norm_stored{i}") for i in range(3)]
        STORED = ("f0", "f1", "fin")

        def stored(norm, tiles, i):
            return 16 * (STORED.index(norm) * (2 if i < 2 else 1) + (tiles + 2 - i) // 3)

        def upto(norm, tiles):
            return NORMS.index(norm) * NT + tiles

        x_rdy = sem("x_ready")
        r_ab = sem("rows_in")
        r_g = sem("gates_in")
        PARTS = [[(0, 16), (16, 48)], [(0, 48)]]
        m_mm, m_add, m_tr, m_cp, m_st = (sem(f"ada_{n}") for n in ("products", "terms", "transposed", "rows", "stored"))

        def part(l, p):
            return len(PARTS[0]) * l + p + 1

        w_in = [[sem(f"w{g}_in{i}") for i in range(3)] for g in range(2)]
        w_used = [sem(f"w{g}_used") for g in range(2)]
        g_mm, g_ed = ({n: sem(f"{n}_{x}") for n in ("win", "uq", "wo0", "vproj", "wo1")} for x in ("done", "taken_dve"))
        g_ea = {n: sem(f"{n}_taken_act") for n in ("win", "uq", "vproj")}
        l_sd, l_rs, l_n, l_tr, l_ta, l_td, l_rope, l_qr, k_rt, k_rc = (sem(n) for n in (
            "lat_sqrt", "lat_rstd", "lat_normed", "lat_transposed", "lat_T_act", "lat_T_dve",
            "k_rope_ready", "q_rope_ready", "krope_transposed", "krope_copied"))
        ATT = (0, 1)
        a_u, a_f = ([sem(f"att{l}_{n}") for l in ATT] for n in ("unit_filled", "unit_free"))
        a_mx, a_ex, a_ri, a_pt, a_pe, a_pv, a_o, o_tr, o_ta, o_td = (sem(f"att_{n}") for n in (
            "max", "exp", "rinv", "pT", "pT_sbuf", "pv", "o", "oT", "oT_act", "oT_dve"))

        def tiles_(l, n):
            return l * H * NT + n

        a_sx = sem("att1_scores_sbuf")
        b_in = [sem(f"bias_in{i}") for i in range(2)]
        b_ok = sem("bias_masked")
        qk_mm, qk_ea, qk_ed = sem("qkT_done"), sem("qkT_act"), sem("qkT_dve")
        kc_in, kc_tr, kc_ta, kc_td = sem("natcache_in"), sem("kcT_transposed"), sem("kcT_act"), sem("kcT_dve")
        ko_tr, ko_ca, ko_cd, ko_out, vs_in = (sem(n) for n in ("kout_transposed", "kout_act", "kout_dve", "kout_stored", "v_shifted"))
        rr_lg, rr_sg, rr_m, rr_cnt, rr_pos, rr_sc, rr_tab = (sem(n) for n in (
            "logits", "scores", "choice", "ranks", "positions", "slots_scattered", "tile_table"))
        e_gw, e_dw, e_inf, e_ys, c_in = ([[sem(f"moe{l}_{n}{i}") for i in range(2)] for l in range(DEPTH)] for n in (
            "gateup_in", "down_in", "info_in", "y_stored", "combine_in"))
        (e_gi, e_tr, e_ta, e_td, e_gu, e_sg, e_ga, e_ac, e_at, e_ae, e_dn, e_ya, e_yd, e_end) = (
            [sem(f"moe{l}_{n}") for l in range(DEPTH)] for n in (
                "rows_in", "rowsT", "rowsT_act", "rowsT_dve", "gateup", "sigmoid", "silu", "acts", "actsT", "actsT_sbuf",
                "down", "y_act", "y_dve", "end"))
        s_out = sem("outputs")
        e_gate = sem("gather_may_start")

        ATT_ADA = [[(0, 6), (0, 7)], [(0, 8), (0, 9)], [(0, 10)], [(0, 11)]] + [[(1, j)] for j in range(12)]
        LOADS = [[("ada", 0, j) for j in range(4)] + [("win", 0, 0), ("win", 0, 1), ("ada", 0, 4), ("ada", 0, 5)]
                 + [("uq", 0, 0), ("uq", 0, 1), ("ukv", 0, 0)] + [("ada", l, j) for hd in ATT_ADA for l, j in hd]
                 + [("wo0", 0, 0), ("wo0", 0, 1)],
                 [("qkv", 0, j) for j in range(6)] + [("wo1", 0, 0), ("wo1", 0, 1)]]

        def source(what, l, j):
            return a["ada"][l, j] if what == "ada" else a["ukv"] if what == "ukv" else a[what][j]

        def w_wait(eng, what, l=0, j=0):
            g = 0 if (what, l, j) in LOADS[0] else 1
            n = LOADS[g].index((what, l, j))
            eng.wait_ge(w_in[g][n % 3], 16 * (n // 3 + 1))
            return n % 3

        UNITS = [("K", 0), ("Q", 0)]
        for h in range(H):
            nxt = h + 1 < H
            UNITS += [("S", h, 0), ("S", h, 1)] + [("K", h + 1)] * nxt + [("S", h, 2)] + [("Q", h + 1)] * nxt
            UNITS += [("S", h, 3), ("S", h, 4)]
        AT = {u: i for i, u in enumerate(UNITS)}
        NS = H * NT

        block = ctx.enter_context(nc.Block())

        @block.sync
        def _(sp):
            sp.dma_start(const[:, :], a["const"]).then_inc(s_const, 16)
            sp.dma_start(vecs[0:112, 0:P], a["vecA"]).then_inc(s_vec, 16)
            sp.dma_start(vecs[0:32, P:2 * P], a["vecB"]).then_inc(s_vec, 16)

            def static_load(g, n):
                if n >= 3:
                    sp.wait_ge(w_used[g], n - 2)
                src = source(*LOADS[g][n])
                slot = n % 3
                sp.dma_start(W[:, slot * 4096:slot * 4096 + src.shape[1]], src).then_inc(w_in[g][slot], 16)

            for n in range(len(LOADS[0])):
                static_load(0, n)
                if n == 6:
                    sp.wait_ge(s_toep, 1)
                    for qc in range(16):
                        sp.dma_start(toepD[qc], toep[:, :, :, 15 - qc:TOEP - qc, :].rearrange("h v r d a -> h (v r) (d a)")).then_inc(s_toepd, 16)
                if n == 1:
                    for t in range(NT):
                        sp.dma_start(x_(t), a["x"][t * P:(t + 1) * P, :]).then_inc(s_x, 16)

            for l in range(DEPTH):
                def load_gu(e, par):
                    sp.dma_start(W[:, par * 4096:(par + 1) * 4096], a["gu"][l][e]).then_inc(e_gw[l][par], 16)

                def load_dn(e, par):
                    at = 2 * 4096 + par * 2048
                    sp.dma_start(W[:, at:at + 2048], a["down"][l][e]).then_inc(e_dw[l][par], 16)

                sp.wait_ge(w_used[l], len(LOADS[l]))
                for k in range(2):
                    load_gu(k, k)
                    load_dn(k, k)
                sp.wait_ge(e_gu[l], 1)
                load_gu(2, 0)
                sp.wait_ge(e_dn[l], 1)
                load_dn(2, 0)
                sp.wait_ge(rr_tab, l + 1)
                pairs = sp.value_load(rtx[0:1, 31:32], min_val=8, max_val=12)
                with sp.Fori(0, pairs - 1) as i:
                    for j in range(2):
                        e = sp.value_load(rtx[0:1, bass.ds(i * 2 + (3 + j), 1)], min_val=0, max_val=E - 1)
                        sp.wait_ge(e_gu[l], i * 2 + (2 + j))
                        load_gu(bass.ds(e, 1), 1 - j)
                        sp.wait_ge(e_dn[l], i * 2 + (2 + j))
                        load_dn(bass.ds(e, 1), 1 - j)
                if l == 0:
                    sp.wait_ge(e_end[l], 1)
                    for n in range(len(LOADS[1])):
                        static_load(1, n)

            sp.wait_ge(s_out, 16 * 3)
            sp.wait_ge(ko_out, 16)

        @block.gpsimd
        def _(pool):
            chain = [0]

            def link(ins):
                chain[0] += 1
                ins.then_inc(s_pool, 1)
                pool.wait_ge(s_pool, chain[0])

            def spread(dst, l, cond, m, sm):
                pool.dma_start(dst, bass.AP(modD.tensor, (l * 96 + cond * 48 + m) * P, [[0, P], [1, D]])).then_inc(sm, 16)

            def rows_in(s, l, m):
                for c in range(2):
                    spread(row(c), l, c, m + 8, r_ab)
                    spread(row(2 + c), l, c, m, r_ab)

            def gates_in(s, l, m):
                for c in range(2):
                    spread(row(4 + c), l, c, m, r_g)

            def rows_out(l, p):
                m0, m1 = PARTS[l][p]
                pool.wait_ge(m_cp, part(l, p))
                for c in range(2):
                    r = l * 96 + c * 48
                    pool.dma_start(modD[r + m0:r + m1, :], modR[c * (m1 - m0):(c + 1) * (m1 - m0), :]).then_inc(m_st, 16)
                pool.wait_ge(m_st, 32 * part(l, p))

            def add_shift(s):
                for t in range(NT):
                    pool.wait_ge(n_ha, upto(s, t + 1))
                    pool.tensor_tensor(HB[t % 3], HB[t % 3], row(2 + t // CTX), ALU.add).then_inc(n_h, 1)
                    if s[0] == "f":
                        pool.wait_ge(n_h, upto(s, t + 1))
                        pool.dma_start(hD[int(s[1])][t * P:(t + 1) * P, :], HB[t % 3]).then_inc(n_st[t % 3], 16)

            pool.dma_start(rpbs.rearrange("h d r -> h (d r)"), a["rpb"]).then_inc(s_rpb, 16)
            pool.memset(zero, 0.0).then_inc(s_zero, 1)
            pool.dma_start(latG[:, 0:QL], bass.AP(a["qnorm"].tensor, 0, [[0, P], [1, QL]])).then_inc(s_par, 16)
            pool.dma_start(latG[:, QL:QL + KVL], bass.AP(a["kvnorm"].tensor, 0, [[0, P], [1, KVL]])).then_inc(s_par, 16)
            pool.dma_start(rt[:, 1320:1320 + E], bass.AP(a["rbias"].tensor, 0, [[0, P], [1, E]])).then_inc(s_par, 16)
            pool.dma_start(wrt[:, :], a["wr"]).then_inc(s_par, 16)
            pool.dma_start(ckc, a["ckv"]).then_inc(s_ck, 16)
            pool.wait_ge(s_zero, 1)
            for l in range(DEPTH):
                pool.dma_start(slotD[l].rearrange("(p n) c -> p (n c)", p=P), zero[:, 0:SLOTS * 2 // P]).then_inc(s_yz, 16)
            for k in range(E + 1, MAXT):
                pool.dma_start(yD[k * P:(k + 1) * P, :], zero).then_inc(s_yz, 16)
            rows_out(0, 0)
            rows_in("m0", 0, 0)
            add_shift("m0")

            pool.dma_start(krw[:, 4, :], a["krope"]).then_inc(s_ck, 16)
            pool.wait_ge(g_ea["win"], 5)
            pool.wait_ge(g_ed["win"], 5)
            pool.dma_start(o["krope"], lat[:, CTX, QL + KVL:IN_DIM]).then_inc(s_out, 16)

            def rotate(src, dst, t, nh):
                cs, sn = (const[:, c + 16 * t:c + 16 * t + 16].rearrange("p (x i) -> p x i", x=2).unsqueeze(1).to_broadcast([P, nh, 2, 8])
                          for c in (C_COS, C_SIN))
                tm = [ropet[:, n, 0:nh] for n in range(4)]
                x1, x2 = src[:, :, :, 0, :], src[:, :, :, 1, :]
                link(pool.tensor_tensor(tm[0], x1, cs, ALU.mult))
                link(pool.tensor_tensor(tm[1], x2, sn, ALU.mult))
                link(pool.tensor_tensor(tm[2], x1, sn, ALU.mult))
                link(pool.tensor_tensor(tm[3], x2, cs, ALU.mult))
                link(pool.tensor_tensor(dst[:, :, :, 0, :], tm[0], tm[1], ALU.subtract))
                return pool.tensor_tensor(dst[:, :, :, 1, :], tm[2], tm[3], ALU.add)

            def halves(v, nh):
                return v.rearrange("p (h x f i) -> p h x f i", h=nh, x=2, f=2)

            for t in range(4):
                link(rotate(halves(lat[:, t, QL + KVL:IN_DIM], 1), halves(krw[:, t, :], 1), t, 1))
            pool.tensor_copy(krw[:, 5, :], lat[:, CTX, QL + KVL:IN_DIM]).then_inc(l_rope, 1)
            pool.wait_ge(l_n, 10)
            pool.dma_start(o["ckv"], lat[:, CTX, QL:QL + KVL]).then_inc(s_out, 16)
            pool.wait_ge(s_out, 32)
            pool.nop().then_inc(l_qr, 1)
            pool.wait_ge(g_ea["uq"], 10)
            pool.wait_ge(g_ed["uq"], 10)
            for t in range(4):
                v = q[:, t, :].rearrange("p (h n) -> p h n", h=H)[:, :, NOPE:QD].rearrange("p h (x f i) -> p h x f i", x=2, f=2)
                link(rotate(v, v, t, H))
            pool.nop().then_inc(l_qr, 1)
            rows_out(0, 1)

            def combine_gathers(l, nxt):
                for t in range(NT):
                    if t >= 2:
                        pool.wait_ge(x_rdy, upto(nxt, t - 1) - NT)
                    for c in range(2):
                        n = 2 * t + c
                        pool.indirect_dma_start(cy[t % 2][c], None, yD, bass.IndirectOffsetOnAxis(ap=rti[:, n:n + 1], axis=0)).then_inc(c_in[l][t % 2], 16)

            def attention_1():
                add_shift("m1")
                pool.dma_start(nvc, a["natv"]).then_inc(kc_in, 16)
                pool.dma_start(kcr, a["natk"]).then_inc(kc_in, 16)
                pool.wait_ge(n_h, upto("m1", NT))
                for i in range(2):
                    link(pool.memset(biasb[i][:, :, LOCAL:], 0.0))

                def bias_tiles(h):
                    b = biasb[h % 2]
                    if h >= 2:
                        pool.wait_ge(a_sx, 4 * (h - 1))
                    for v in range(3):
                        off = (h * 2 + (v == 1)) * ROWS * TLEN + (TSTART[v] - 15) * ROWS
                        src = bass.AP(toepD.tensor, off, [[H * 2 * ROWS * TLEN, 16], [TLEN, ROWS], [1, LOCAL]])
                        pool.dma_start(b[:, v, 0:LOCAL], src).then_inc(b_in[h % 2], 16)
                    pool.wait_ge(b_in[h % 2], 48 * (h // 2 + 1))
                    for n, v in enumerate((0, 2)):
                        mask = const[:, C_MASK + n * LOCAL:C_MASK + (n + 1) * LOCAL]
                        pool.tensor_tensor(b[:, v, 0:LOCAL], b[:, v, 0:LOCAL], mask, ALU.add).then_inc(b_ok, 1)

                pool.wait_ge(s_toepd, 16 * 16)
                bias_tiles(0)
                bias_tiles(1)
                pool.wait_ge(ko_ca, 1)
                pool.wait_ge(ko_cd, 1)
                pool.dma_start(o["k"], kout).then_inc(ko_out, 16)
                pool.wait_ge(g_ea["vproj"], 5)
                pool.wait_ge(g_ed["vproj"], 5)
                pool.dma_start(o["v"], nv[:, CTX, :]).then_inc(s_out, 16)
                pool.wait_ge(ko_out, 16)
                for i in range(3):
                    pool.dma_start(nvs[0:64, i, :], nv[64:128, i, :]).then_inc(vs_in, 16)
                    pool.dma_start(nvs[64:128, i, :], nv[0:64, i + 1, :]).then_inc(vs_in, 16)
                for h in range(2, H):
                    bias_tiles(h)

            pay = rt[:, 1290:1310]
            for l in range(DEPTH):
                if l == 1:
                    attention_1()
                s = f"f{l}"
                pool.wait_ge(o_tr, KD * l + KD)
                if l == 0:
                    gates_in("m0", 0, 16)
                rows_in(s, l, 24)
                add_shift(s)
                if l == 0:
                    rows_out(1, 0)
                pool.wait_ge(x_rdy, upto(s, NT) - NT)
                gates_in(s, l, 40)
                if l == 0:
                    pool.wait_ge(n_h, upto(s, NT))
                    rows_in("m1", 1, 0)
                for i in range(3):
                    pool.wait_ge(n_st[i], stored(s, NT, i))
                pool.wait_ge(s_yz, 16 * (2 + XTILES - 1))
                pool.wait_ge(rr_pos, l + 1)
                for t in range(NT):
                    for c in range(2):
                        n = 2 * t + c
                        pool.indirect_dma_start(slotD[l], bass.IndirectOffsetOnAxis(ap=rti[:, n:n + 1], axis=0),
                                                pay[:, 2 * n:2 * n + 2], None).then_inc(rr_sc, 16)
                pool.wait_ge(rr_sc, 160 * (l + 1))
                pool.wait_ge(rr_tab, l + 1)
                pairs = pool.value_load(rtx[0:1, 31:32], min_val=8, max_val=12)

                def info_in(rows, par):
                    pool.dma_start(info[:, 2 * par:2 * par + 2], slotD[l][rows, :]).then_inc(e_inf[l][par], 16)

                def rows_of(par):
                    pool.indirect_dma_start(gat, None, hD[l], bass.IndirectOffsetOnAxis(
                        ap=info[:, 2 * par:2 * par + 1].bitcast(U32), axis=0)).then_inc(e_gi[l], 16)

                info_in(slice(0, P), 0)
                info_in(slice(P, 2 * P), 1)
                pool.wait_ge(e_inf[l][0], 16)
                rows_of(0)
                pool.wait_ge(e_inf[l][1], 16)
                pool.wait_ge(e_tr[l], 1)
                rows_of(1)
                with pool.Fori(0, pairs) as i:
                    for j in range(2):
                        pool.wait_ge(e_ac[l], i * 2 + (1 + j))
                        info_in(bass.ds(i * (2 * P) + (2 + j) * P, P), j)
                        pool.wait_ge(e_inf[l][j], i * 16 + 32)
                        pool.wait_ge(e_tr[l], i * 2 + (2 + j))
                        pool.nop().then_inc(e_gate, 1)
                        rows_of(j)
                pool.wait_ge(e_ys[l][0], pairs * 16 + 32)
                pool.wait_ge(e_ys[l][1], pairs * 16 + 16)
                pool.nop().then_inc(e_gate, 1)
                combine_gathers(l, "m1" if l == 0 else "fin")
                if l == 0:
                    pool.wait_ge(x_rdy, upto("m1", NT) - NT)
                    gates_in("m1", 1, 16)
                else:
                    pool.wait_ge(n_h, upto("f1", NT))
                    pool.dma_start(row(0), bass.AP(a["gfin"].tensor, 0, [[0, P], [1, D]])).then_inc(r_ab, 16)
            for t in range(NT):
                pool.wait_ge(n_ha, upto("fin", t + 1))
                pool.dma_start(o["y"][t * P:(t + 1) * P, :], HB[t % 3]).then_inc(n_st[t % 3], 16)
            for i in range(3):
                pool.wait_ge(n_st[i], stored("fin", NT, i))

        @block.tensor
        def _(pe):
            def transpose(dst, src, n=P):
                return pe.transpose(dst, src, const[0:n, C_ID:C_ID + n])

            def ada(l, j):
                slot = w_wait(pe, "ada", l, j)
                w = w_(slot, KD, 512)
                for mm in range(4):
                    m = l * 96 + 4 * j + mm
                    for k in range(KD):
                        ins = pe.matmul(PS[:, 7 * 512 + m:7 * 512 + m + 49:48], w[:, k, mm * P:(mm + 1) * P], condT[:, 2 * k:2 * k + 2],
                                        start=(k == 0), stop=(k == KD - 1))
                ins.then_inc(w_used[0], 1)
                for p, (m0, m1) in enumerate(PARTS[l]):
                    if 4 * j + 4 == m1:
                        pe.wait_ge(w_used[0], [n for n, x in enumerate(LOADS[0]) if x == ("ada", l, j)][0] + 1)
                        pe.nop().then_inc(m_mm, 1)

            def ada_rows(l, p, b):
                m0, m1 = PARTS[l][p]
                n = 2 * (m1 - m0)
                pe.wait_ge(m_add, part(l, p))
                v = modT[:, l * 96 + 2 * m0:l * 96 + 2 * m1]
                pe.transpose(PS[0:n, b * 512 + 256:b * 512 + 384], v, ident).then_inc(m_tr, 1)

            def norm_transposes(s):
                for t in range(NT):
                    pe.wait_ge(n_h, upto(s, t + 1))
                    if t >= 2:
                        pe.wait_ge(n_ta, upto(s, t - 1))
                        pe.wait_ge(n_td, upto(s, t - 1))
                    for c in range(KD):
                        ins = transpose(bank(2 * (t % 2), P, c * P), HB[t % 3][:, c * P:(c + 1) * P])
                    ins.then_inc(n_tr, 1)
                    if s[0] == "f":
                        pe.wait_ge(n_ta, upto(s, t + 1))
                        pe.wait_ge(n_td, upto(s, t + 1))
                        if t == 0:
                            pe.wait_ge(s_par, 64)
                        for k in range(KD):
                            ins = pe.matmul(bank(6, E, t * E), hT[:, k, t * P:(t + 1) * P], wrt[:, k * E:(k + 1) * E],
                                            start=(k == 0), stop=(k == KD - 1))
                        ins.then_inc(rr_lg, 1)

            def gemm_unit(name, u, n, ks, lhs, rhs, done=None):
                if u >= 2:
                    pe.wait_ge(g_ea[name] if u % 2 == 0 else g_ed[name], u // 2)
                for k in range(ks):
                    ins = pe.matmul(bank(4 + u % 2, n), lhs(k), rhs(k), start=(k == 0), stop=(k == ks - 1))
                ins.then_inc(g_mm[name], 1)

            pe.wait_ge(s_const, 16)
            pe.wait_ge(s_vec, 32)
            pe.transpose(bank(6, 112), vecs[0:112, 0:P], const[0:112, C_ID:C_ID + 112])
            pe.transpose(bank(6, 32, 112), vecs[0:32, P:2 * P], const[0:32, C_ID:C_ID + 32]).then_inc(s_vt, 1)
            pe.wait_ge(s_cond, 1)
            for j in range(4):
                ada(0, j)
            ada_rows(0, 0, 6)
            norm_transposes("m0")

            pe.wait_ge(n_ta, upto("m0", NT))
            pe.wait_ge(n_td, upto("m0", NT))
            for j in range(2):
                w = w_(w_wait(pe, "win", 0, j), KD, 336)
                for t in range(NT):
                    gemm_unit("win", j * NT + t, 336, KD, lambda k: hT[:, k, t * P:(t + 1) * P], lambda k: w[:, k, :])
                pe.wait_ge(g_mm["win"], (j + 1) * NT)
                pe.nop().then_inc(w_used[0], 1)
            ada(0, 4)
            ada(0, 5)
            pe.wait_ge(s_ck, 32)
            for t in range(6):
                if t < NT:
                    pe.wait_ge(l_n, 2 * t + 2)
                if t >= 2:
                    pe.wait_ge(l_ta, t - 1)
                    pe.wait_ge(l_td, t - 1)
                b = 2 * (t % 2)
                if t < NT:
                    for c in range(3):
                        transpose(bank(b, P, c * P), lat[:, t, c * P:(c + 1) * P])
                for c in range(2):
                    src = lat[:, t, QL + c * P:QL + (c + 1) * P] if t < NT else ckc[:, c * P:(c + 1) * P]
                    ins = transpose(bank(b + 1, P, c * P), src)
                ins.then_inc(l_tr, 1)
            pe.wait_ge(l_rope, 1)
            pe.wait_ge(l_ta, 5)
            pe.wait_ge(l_td, 6)
            for kt in range(6):
                ins = transpose(PS[0:ROPE, kt * P:(kt + 1) * P], krw[:, kt, :])
            ins.then_inc(k_rt, 1)
            for j in range(2):
                w = w_(w_wait(pe, "uq", 0, j), 3, 768)
                for n in range(2):
                    for t in range(NT):
                        gemm_unit("uq", (j * 2 + n) * NT + t, 384, 3, lambda k: cqT[:, k, t * P:(t + 1) * P],
                                  lambda k: w[:, k, n * 384:(n + 1) * 384])
                pe.wait_ge(g_mm["uq"], (j + 1) * 10)
                pe.nop().then_inc(w_used[0], 1)
            w = w_(w_wait(pe, "ukv"), 2, 2048)
            for kt in range(6):
                for n in range(4):
                    gemm_unit("uq", 20 + kt * 4 + n, 512, 2, lambda k: ckvT[:, k, kt * P:(kt + 1) * P],
                              lambda k: w[:, k, n * 512:(n + 1) * 512])
            pe.wait_ge(g_mm["uq"], 44)
            pe.nop().then_inc(w_used[0], 1)

            def mla_pT(s):
                pe.wait_ge(a_ex, tiles_(0, s + 1))
                if s >= 1:
                    pe.wait_ge(a_pe, tiles_(0, s))
                n = NT if s % NT < CTX else 1
                for c in range(n):
                    ins = transpose(bank(4, P, c * P), Pm[s % 2][:, c * P:(c + 1) * P])
                ins.then_inc(a_pt, 1)

            def mla_pv(s):
                h, t = divmod(s, NT)
                pe.wait_ge(a_pe, tiles_(0, s + 1))
                if s >= 1:
                    pe.wait_ge(a_o, tiles_(0, s))
                tiles = list(range(5)) if t < CTX else [5]
                for c, kt in enumerate(tiles):
                    ins = pe.matmul(bank(6, VD), PTm[s % 2][:, c * P:(c + 1) * P], mv[:, kt, h * VD:(h + 1) * VD],
                                    start=(c == 0), stop=(c == len(tiles) - 1))
                ins.then_inc(a_pv, 1)

            pe.wait_ge(k_rc, 1)
            pe.wait_ge(g_ea["uq"], 22)
            pe.wait_ge(g_ed["uq"], 22)
            pe.wait_ge(l_qr, 2)
            for i, u in enumerate(UNITS):
                b = 2 * (i % 2)
                if i >= 2:
                    pe.wait_ge(a_f[0], i - 1)
                h = u[1]
                if u[0] == "K":
                    for kt in range(6):
                        ins = transpose(PS[0:NOPE, b * 512 + kt * P:b * 512 + (kt + 1) * P], kn[:, kt, h * NOPE:(h + 1) * NOPE])
                    ins.then_inc(a_u[0], 1)
                elif u[0] == "Q":
                    for t in range(NT):
                        ins = transpose(PS[0:QD, b * 512 + t * P:b * 512 + (t + 1) * P], q[:, t, h * QD:(h + 1) * QD])
                    ins.then_inc(a_u[0], 1)
                else:
                    t, s = u[2], h * NT + u[2]
                    if t == 0:
                        pe.wait_ge(a_f[0], max(AT["Q", h], AT["K", h]) + 1)
                    lhs = qTh[h % 2][0:QD, t * P:(t + 1) * P]
                    if t < CTX:
                        pe.matmul(bank(b), lhs, kTh[h % 2][0:QD, 0:512], start=True, stop=True)
                        ins = pe.matmul(bank(b + 1, P), lhs, kTh[h % 2][0:QD, 512:640], start=True, stop=True)
                    else:
                        ins = pe.matmul(bank(b, P), lhs, kTh[h % 2][0:QD, 640:768], start=True, stop=True)
                    ins.then_inc(a_u[0], 1)
                    if s >= 1:
                        mla_pT(s - 1)
                    if s >= 2:
                        mla_pv(s - 2)
                    if (h, t) == (4, 1):
                        ada_rows(0, 1, 7)
                    if t == CTX:
                        for l, j in ATT_ADA[h]:
                            if (l, j) == (1, 0):
                                pe.wait_ge(m_cp, part(0, 1))
                            ada(l, j)
            mla_pT(NS - 1)
            mla_pv(NS - 2)
            mla_pv(NS - 1)

            def out_projection(l):
                for c in range(KD):
                    if c == 0:
                        pe.wait_ge(a_o, tiles_(l, NS))
                    if c >= 2:
                        pe.wait_ge(o_td if c % 2 else o_ta, 4 * l + c // 2)
                    b = 2 * (c % 2)
                    for t in range(NT):
                        ins = transpose(bank(b, P, t * P), O[:, t, c * P:(c + 1) * P])
                    ins.then_inc(o_tr, 1)
                name = f"wo{l}"
                w = [w_(w_wait(pe, name, 0, j), KD, 512) for j in range(2)]
                pe.wait_ge(o_ta, 4 * l + 4)
                pe.wait_ge(o_td, 4 * l + 4)
                for t in range(NT):
                    for j in range(2):
                        u = 2 * t + j
                        if u >= 2:
                            pe.wait_ge(g_ed[name], u - 1)
                        for k in range(KD):
                            ins = pe.matmul(bank(4 + j), OT[:, k, t * P:(t + 1) * P], w[j][:, k, :], start=(k == 0), stop=(k == KD - 1))
                        ins.then_inc(g_mm[name], 1)
                pe.wait_ge(g_mm[name], 2 * NT)
                pe.nop().then_inc(w_used[l], 2)

            def routing(l):
                pe.wait_ge(rr_m, l + 1)
                M = [rt[:, 480 + t * E:480 + (t + 1) * E] for t in range(NT)]
                for t in range(NT):
                    for tt in range(t + 1):
                        pe.matmul(bank(7, E, t * E), tri if tt == t else ones, M[tt], start=(tt == 0), stop=(tt == t))
                for t in range(NT):
                    ins = pe.matmul(bank(7, E, NT * E), ones, M[t], start=(t == 0), stop=(t == NT - 1))
                ins.then_inc(rr_cnt, 1)

            def moe(l):
                pairs = None

                def rows_T(gi):
                    pe.wait_ge(e_gi[l], gi)
                    for c in range(KD):
                        ins = transpose(bank(3, P, c * P), gat[:, c * P:(c + 1) * P])
                    ins.then_inc(e_tr[l], 1)

                def gateup(par, w_ready, rows_ready):
                    pe.wait_ge(e_gw[l][par], w_ready)
                    pe.wait_ge(e_ta[l], rows_ready)
                    pe.wait_ge(e_td[l], rows_ready)
                    w = w_(par, KD, 512)
                    for k in range(KD):
                        ins = pe.matmul(bank(0), gatT[:, k, :], w[:, k, :], start=(k == 0), stop=(k == KD - 1))
                    ins.then_inc(e_gu[l], 1)

                def acts_T(ready):
                    pe.wait_ge(e_ac[l], ready)
                    for c in range(2):
                        ins = transpose(bank(5, P, c * P), actv[:, c * P:(c + 1) * P])
                    ins.then_inc(e_at[l], 1)

                def down(par, w_ready, acts_ready, free):
                    pe.wait_ge(e_dw[l][par], w_ready)
                    pe.wait_ge(e_ae[l], acts_ready)
                    pe.wait_ge(e_ya[l], free)
                    pe.wait_ge(e_yd[l], free)
                    w = W[:, 8192 + par * 2048:8192 + (par + 1) * 2048].rearrange("p (k n) -> p k n", k=2)
                    for n in range(2):
                        for k in range(2):
                            ins = pe.matmul(bank(1 + n), actT[:, k, :], w[:, k, n * 512:(n + 1) * 512], start=(k == 0), stop=(k == 1))
                    ins.then_inc(e_dn[l], 1)

                rows_T(16)
                gateup(0, 16, 1)
                rows_T(32)
                acts_T(1)
                pe.wait_ge(rr_tab, l + 1)
                pairs = pe.value_load(rtx[0:1, 31:32], min_val=8, max_val=12)
                with pe.Fori(0, pairs) as i:
                    for j in range(2):
                        par = 1 - j
                        gateup(par, i * 16 + 16 * (1 + j), i * 2 + (2 + j))
                        rows_T(i * 32 + 16 * (3 + j))
                        down(1 - par, i * 16 + 16, i * 2 + (1 + j), i * 2 + (1 + j))
                        acts_T(i * 2 + (2 + j))
                down(0, pairs * 16 + 16, pairs * 2 + 1, pairs * 2 + 1)
                pe.wait_ge(e_dn[l], pairs * 2 + 1)
                pe.nop().then_inc(e_end[l], 1)

            out_projection(0)
            ada_rows(1, 0, 7)
            norm_transposes("f0")
            pe.wait_ge(m_cp, part(1, 0))
            routing(0)
            moe(0)

            norm_transposes("m1")
            pe.wait_ge(kc_in, 32)
            pe.wait_ge(n_ta, upto("m1", NT))
            pe.wait_ge(n_td, upto("m1", NT))
            for c in range(KD):
                ins = transpose(bank(0, P, c * P), kcr[:, c * P:(c + 1) * P])
            ins.then_inc(kc_tr, 1)
            for u in range(16):
                if u % 4 == 0:
                    w = w_(w_wait(pe, "qkv", 0, u // 4), KD, 512)
                if u == 1:
                    pe.wait_ge(kc_ta, 1)
                    pe.wait_ge(kc_td, 1)
                if u >= 2:
                    pe.wait_ge(qk_ea if u % 2 == 0 else qk_ed, u // 2)
                b = (2, 0)[u % 2]
                m = u % 4
                for n0, n1, bb in ((0, 512, b), (512, 640, b + 1)):
                    for k in range(KD):
                        ins = pe.matmul(bank(bb, n1 - n0), w[:, k, m * P:(m + 1) * P], hT[:, k, n0:n1], start=(k == 0), stop=(k == KD - 1))
                ins.then_inc(qk_mm, 1)
                if u % 4 == 3:
                    pe.wait_ge(qk_mm, u + 1)
                    pe.nop().then_inc(w_used[1], 1)
            for j in range(2):
                w = w_(w_wait(pe, "qkv", 0, 4 + j), KD, 512)
                for t in range(NT):
                    gemm_unit("vproj", j * NT + t, 512, KD, lambda k: hT[:, k, t * P:(t + 1) * P], lambda k: w[:, k, :])
                if j == 0:
                    pe.wait_ge(qk_ea, 8)
                    pe.wait_ge(qk_ed, 8)
                    for c in range(KD):
                        ins = transpose(bank(0, P, c * P), kT[:, c, 512:640])
                    ins.then_inc(ko_tr, 1)
                pe.wait_ge(g_mm["vproj"], (j + 1) * NT)
                pe.nop().then_inc(w_used[1], 1)

            def nat_scores(s):
                h, t = divmod(s, NT)
                if s >= 4:
                    pe.wait_ge(a_f[1], s - 3)
                r, hp = (h % 2) * 64, h // 2
                lhs = qT[r:r + 64, hp, t * P:(t + 1) * P]
                if t < CTX:
                    pe.matmul(bank(s % 4, LOCAL), lhs, kT[r:r + 64, hp, KEY0[t]:KEY0[t] + LOCAL], start=True, stop=True)
                    ins = pe.matmul(bank(s % 4, P, LOCAL), lhs, kcT[r:r + 64, hp, :], start=True, stop=True)
                else:
                    ins = pe.matmul(bank(s % 4, P), lhs, kT[r:r + 64, hp, 512:640], start=True, stop=True)
                ins.then_inc(a_u[1], 1)

            def nat_pT(s):
                pe.wait_ge(a_ex, tiles_(1, s + 1))
                if s >= 2:
                    pe.wait_ge(a_pe, tiles_(1, s - 1))
                for c in range(3 if s % NT < CTX else 1):
                    ins = transpose(bank(4 + s % 2, P, c * P), Pn[s % 2][:, c * P:(c + 1) * P])
                ins.then_inc(a_pt, 1)

            def nat_pv(s):
                h, t = divmod(s, NT)
                pe.wait_ge(a_pe, tiles_(1, s + 1))
                if s >= 1:
                    pe.wait_ge(a_o, tiles_(1, s))
                cols = slice(h * VD, (h + 1) * VD)
                cache = nvc[:, cols]
                vals = [[nv[:, 0, cols], nv[:, 1, cols], cache], [nvs[:, 0, cols], nvs[:, 1, cols], cache],
                        [nvs[:, 1, cols], nvs[:, 2, cols], cache], [nv[:, 2, cols], nv[:, 3, cols], cache], [nv[:, 4, cols]]][t]
                for c, v in enumerate(vals):
                    ins = pe.matmul(bank(6, VD), PTn[s % 2][:, c * P:(c + 1) * P], v, start=(c == 0), stop=(c == len(vals) - 1))
                ins.then_inc(a_pv, 1)

            pe.wait_ge(ko_ca, 1)
            pe.wait_ge(ko_cd, 1)
            pe.wait_ge(g_ea["vproj"], 5)
            pe.wait_ge(g_ed["vproj"], 5)
            for s in range(NS + 3):
                if s < NS:
                    nat_scores(s)
                if s == 3:
                    pe.wait_ge(vs_in, 96)
                if 2 <= s < NS + 2:
                    nat_pT(s - 2)
                if s >= 3:
                    nat_pv(s - 3)
            out_projection(1)
            norm_transposes("f1")
            routing(1)
            moe(1)

        @block.scalar
        def _(act):
            chain = [0]

            def link(ins):
                chain[0] += 1
                ins.then_inc(s_act, 1)
                act.wait_ge(s_act, chain[0])

            def norm(s):
                i = NORMS.index(s)
                ss, sd, rs = (st[:, n + 5 * i:n + 5 * i + 5] for n in (0, 25, 50))
                for t in range(NT + 2):
                    if t < NT:
                        if s == "m0":
                            act.wait_ge(s_x, 16 * NT)
                        else:
                            act.wait_ge(x_rdy, upto(s, t + 1) - NT)
                        if t >= 3:
                            if s != "fin":
                                act.wait_ge(n_tr, upto(s, t - 2))
                            if s in STORED:
                                act.wait_ge(n_st[t % 3], stored(s, t - 2, t % 3))
                        link(act.activation(HB[t % 3], x_(t), ACT.Square, accum_out=ss[:, t:t + 1]))
                        act.activation(sd[:, t:t + 1], ss[:, t:t + 1], ACT.Sqrt, scale=1.0 / D, bias=const[:, C_EPS:C_EPS + 1]).then_inc(n_sd, 1)
                    if 1 <= t <= NT:
                        act.wait_ge(n_rs, upto(s, t))
                        act.activation(HB[(t - 1) % 3], x_(t - 1), ACT.Copy, scale=rs[:, t - 1:t]).then_inc(n_xn, 1)
                    if t >= 2 and s != "fin":
                        act.wait_ge(n_tr, upto(s, t - 1))
                        act.activation(hT[:, 0:4, (t - 2) * P:(t - 1) * P], bank(2 * (t % 2)).rearrange("p (c n) -> p c n", c=4),
                                       ACT.Copy).then_inc(n_ta, 1)

            act.wait_ge(s_vc, 1)
            act.activation(st[:, 144:160], vecT[:, 96:112], ACT.Sigmoid).then_inc(s_sg, 1)
            act.wait_ge(s_const, 16)
            norm("m0")

            for u in range(0, 10, 2):
                act.wait_ge(g_mm["win"], u + 1)
                act.activation(lat[:, u % NT, u // NT * 336:(u // NT + 1) * 336], bank(4, 336), ACT.Copy).then_inc(g_ea["win"], 1)
            act.wait_ge(g_ea["win"], 5)
            act.wait_ge(g_ed["win"], 5)
            junk = R[:, 0:QL]
            act.wait_ge(n_h, upto("m0", NT))
            for t in range(NT):
                link(act.activation(junk, lat[:, t, 0:QL], ACT.Square, accum_out=st[:, 80 + t:81 + t]))
                link(act.activation(junk[:, 0:KVL], lat[:, t, QL:QL + KVL], ACT.Square, accum_out=st[:, 85 + t:86 + t]))
            act.activation(st[:, 90:95], st[:, 80:85], ACT.Sqrt, scale=1.0 / QL, bias=const[:, C_EPS:C_EPS + 1]).then_inc(l_sd, 1)
            act.activation(st[:, 95:100], st[:, 85:90], ACT.Sqrt, scale=1.0 / KVL, bias=const[:, C_EPS:C_EPS + 1]).then_inc(l_sd, 1)
            for t in range(NT):
                act.wait_ge(l_tr, t + 1)
                act.activation(cqT[:, :, t * P:(t + 1) * P], bank(2 * (t % 2), QL).rearrange("p (c n) -> p c n", c=3), ACT.Copy).then_inc(l_ta, 1)
            act.wait_ge(k_rt, 1)
            link(act.activation(kTh[0][NOPE:QD, :], PS[0:ROPE, 0:768], ACT.Copy))
            act.activation(kTh[1][NOPE:QD, :], PS[0:ROPE, 0:768], ACT.Copy).then_inc(k_rc, 1)
            act.wait_ge(l_qr, 1)
            act.wait_ge(s_yz, 16 * (2 + XTILES - 1))
            for u in range(0, 20, 2):
                act.wait_ge(g_mm["uq"], u + 1)
                n, t = divmod(u, NT)
                act.activation(q[:, t, n * 384:(n + 1) * 384], bank(4, 384), ACT.Copy, scale=MLA_SCALE).then_inc(g_ea["uq"], 1)
            act.wait_ge(s_toepd, 16 * 16)
            for u in range(0, 24, 2):
                act.wait_ge(g_mm["uq"], 20 + u + 1)
                kt, n = divmod(u, 4)
                src = bank(4).rearrange("p (h c) -> p h c", h=4)
                act.activation(kn[:, kt, n * 256:(n + 1) * 256].rearrange("p (h c) -> p h c", h=4), src[:, :, 0:NOPE], ACT.Copy)
                act.activation(mv[:, kt, n * 256:(n + 1) * 256].rearrange("p (h c) -> p h c", h=4), src[:, :, NOPE:], ACT.Copy).then_inc(g_ea["uq"], 1)

            def o_out(l, s):
                h, t = divmod(s, NT)
                act.wait_ge(a_pv, tiles_(l, s + 1))
                act.wait_ge(a_ri, tiles_(l, s + 1))
                act.activation(O[:, t, h * VD:(h + 1) * VD], bank(6, VD), ACT.Copy, scale=st[:, 108 + s % 4:109 + s % 4]).then_inc(a_o, 1)

            for i, u in enumerate(UNITS):
                b = 2 * (i % 2)
                h = u[1]
                act.wait_ge(a_u[0], i + 1)
                if u[0] == "K":
                    act.activation(kTh[h % 2][0:NOPE, :], PS[0:NOPE, b * 512:b * 512 + 768], ACT.Copy).then_inc(a_f[0], 1)
                elif u[0] == "Q":
                    act.activation(qTh[h % 2][0:QD, :], PS[0:QD, b * 512:b * 512 + 640], ACT.Copy).then_inc(a_f[0], 1)
                else:
                    s = h * NT + u[2]
                    n = 640 if u[2] < CTX else P
                    act.wait_ge(a_mx, tiles_(0, s + 1))
                    if s >= 2:
                        act.wait_ge(a_pt, tiles_(0, s - 1))
                    if s >= 4:
                        act.wait_ge(a_ri, tiles_(0, s - 3))
                    act.activation(Pm[s % 2][:, 0:n], bank(b, n), ACT.Exp, bias=st[:, 100 + s % 4:101 + s % 4],
                                   accum_out=st[:, 104 + s % 4:105 + s % 4]).then_inc(a_ex, 1)
                    act.wait_ge(a_ex, tiles_(0, s + 1))
                    act.nop().then_inc(a_f[0], 1)
                    if s >= 2:
                        o_out(0, s - 2)
            o_out(0, NS - 2)
            o_out(0, NS - 1)

            def oT_half(l):
                for c in range(0, KD, 2):
                    act.wait_ge(o_tr, KD * l + c + 1)
                    act.activation(OT[:, c, :], bank(0, 640), ACT.Copy).then_inc(o_ta, 1)

            def scores(l):
                act.wait_ge(rr_lg, NT * (l + 1))
                act.activation(rt[:, 0:80], bank(6, 80), ACT.Sigmoid).then_inc(rr_sg, 1)

            def moe(l):
                def rows_T(ready):
                    act.wait_ge(e_tr[l], ready)
                    act.activation(gatT[:, 0:4, :], bank(3).rearrange("p (c n) -> p c n", c=4), ACT.Copy).then_inc(e_ta[l], 1)

                def sigmoid(ready, free):
                    act.wait_ge(e_gu[l], ready)
                    if free is not None:
                        act.wait_ge(e_ga[l], free)
                    act.activation(sig, bank(0, DE), ACT.Sigmoid).then_inc(e_sg[l], 1)

                def y_out(ready, par, free, rows):
                    act.wait_ge(e_dn[l], ready)
                    act.wait_ge(e_ys[l][par], free)
                    act.activation(yb[par][:, 0:512], bank(1), ACT.Copy).then_inc(e_ya[l], 1)
                    act.wait_ge(e_ya[l], ready + 1)
                    act.wait_ge(e_yd[l], ready + 1)
                    act.dma_start(yD[rows, :], yb[par]).then_inc(e_ys[l][par], 16)

                act.nop().then_inc(e_ya[l], 1)
                for p in range(2):
                    act.nop().then_inc(e_ys[l][p], 16)
                rows_T(1)
                sigmoid(1, None)
                rows_T(2)
                act.wait_ge(rr_tab, l + 1)
                pairs = act.value_load(rtx[0:1, 31:32], min_val=8, max_val=12)
                with act.Fori(0, pairs) as i:
                    for j in range(2):
                        sigmoid(i * 2 + (2 + j), i * 2 + (1 + j))
                        rows_T(i * 2 + (3 + j))
                        y_out(i * 2 + (1 + j), j, i * 16 + 16, bass.ds(i * (2 * P) + j * P, P))
                y_out(pairs * 2 + 1, 0, pairs * 16 + 16, bass.ds(pairs * (2 * P), P))

            oT_half(0)
            norm("f0")
            scores(0)
            moe(0)

            norm("m1")
            act.wait_ge(kc_tr, 1)
            act.activation(kcT[:, 0:4, :], bank(0).rearrange("p (c n) -> p c n", c=4), ACT.Copy).then_inc(kc_ta, 1)
            for u in range(0, 16, 2):
                act.wait_ge(qk_mm, u + 1)
                dst = qT[:, u, :] if u < 8 else kT[:, u - 8, :]
                act.activation(dst, bank(2, 640), ACT.Copy, scale=NAT_SCALE if u < 8 else 1.0).then_inc(qk_ea, 1)

            def v_out(u):
                act.wait_ge(g_mm["vproj"], u + 1)
                j, t = divmod(u, NT)
                act.activation(nv[:, t, j * 512:(j + 1) * 512], bank(4), ACT.Copy).then_inc(g_ea["vproj"], 1)

            for u in (0, 2, 4):
                v_out(u)
            act.wait_ge(ko_tr, 1)
            act.activation(kout[:, 0:512], bank(0), ACT.Copy).then_inc(ko_ca, 1)
            for u in (6, 8):
                v_out(u)
            for s in range(NS + 3):
                if s < NS:
                    t = s % NT
                    act.wait_ge(a_mx, tiles_(1, s + 1))
                    if s >= 4:
                        act.wait_ge(a_ri, tiles_(1, s - 3))
                    if t < CTX:
                        src, n = Pn[s % 2], 384
                    else:
                        src, n = bank(s % 4, P), P
                        if s >= 2:
                            act.wait_ge(a_pt, tiles_(1, s - 1))
                    act.activation(Pn[s % 2][:, 0:n], src, ACT.Exp, bias=st[:, 100 + s % 4:101 + s % 4],
                                   accum_out=st[:, 104 + s % 4:105 + s % 4]).then_inc(a_ex, 1)
                if s >= 3:
                    o_out(1, s - 3)
            oT_half(1)
            norm("f1")
            scores(1)
            moe(1)
            norm("fin")

        @block.vector
        def _(dve):
            chain = [0]

            def link(ins):
                chain[0] += 1
                ins.then_inc(s_dve, 1)
                dve.wait_ge(s_dve, chain[0])

            def tt(dst, x, y, op):
                return dve.tensor_tensor(dst, x, y, op)

            def norm(s):
                i = NORMS.index(s)
                sd, rs = (st[:, n + 5 * i:n + 5 * i + 5] for n in (25, 50))
                for t in range(NT + 2):
                    if t < NT:
                        dve.wait_ge(n_sd, upto(s, t + 1))
                        dve.reciprocal(rs[:, t:t + 1], sd[:, t:t + 1]).then_inc(n_rs, 1)
                    if 1 <= t <= NT:
                        c = (t - 1) // CTX if s != "fin" else 0
                        if t == 1:
                            dve.wait_ge(r_ab, 64 * (i + 1) if s != "fin" else 64 * 4 + 16)
                        dve.wait_ge(n_xn, upto(s, t))
                        tt(HB[(t - 1) % 3], HB[(t - 1) % 3], row(c), ALU.mult).then_inc(n_ha, 1)
                    if t >= 2 and s != "fin":
                        dve.wait_ge(n_tr, upto(s, t - 1))
                        dve.tensor_copy(hT[:, 4:8, (t - 2) * P:(t - 1) * P],
                                        bank(2 * (t % 2) + 1).rearrange("p (c n) -> p c n", c=4)).then_inc(n_td, 1)

            def ada_terms(l, p):
                m0, m1 = PARTS[l][p]
                dve.wait_ge(m_mm, part(l, p))
                v = modT[:, l * 96 + 2 * m0:l * 96 + 2 * m1].rearrange("p (c m) -> p c m", c=2)
                ps = bank(7, 96, l * 96).rearrange("p (c m) -> p c m", c=2)
                n = m1 - m0
                link(tt(v, ps[:, :, m0:m1], vecT[:, l * 48 + m0:l * 48 + m1].unsqueeze(1).to_broadcast([P, 2, n]), ALU.add))
                todo = [(m - m0, g) for m, g in ((8, 112 + l * 8), (32, 128 + l * 8)) if m0 <= m < m1]
                for i, (m, g) in enumerate(todo):
                    ins = dve.scalar_tensor_tensor(out=v[:, :, m:m + 8], in0=v[:, :, m:m + 8], scalar=1.0,
                                                   in1=vecT[:, g:g + 8].unsqueeze(1).to_broadcast([P, 2, 8]), op0=ALU.add, op1=ALU.mult)
                    link(ins)
                dve.nop().then_inc(m_add, 1)

            def ada_rows(l, p, b):
                m0, m1 = PARTS[l][p]
                n = 2 * (m1 - m0)
                dve.wait_ge(m_tr, part(l, p))
                if (l, p) != (0, 0):
                    dve.wait_ge(m_st, 32 * (part(l, p) - 1))
                dve.tensor_copy(modR[0:n, :], PS[0:n, b * 512 + 256:b * 512 + 384]).then_inc(m_cp, 1)

            dve.wait_ge(s_vt, 1)
            dve.tensor_copy(vecT[:, :], bank(6, 144)).then_inc(s_vc, 1)
            dve.wait_ge(s_vc, 1)
            dve.wait_ge(s_sg, 1)
            tt(condT[:, :].rearrange("p (k c) -> p c k", c=2), vecT[:, 96:112].rearrange("p (c k) -> p c k", c=2),
               st[:, 144:160].rearrange("p (c k) -> p c k", c=2), ALU.mult).then_inc(s_cond, 1)
            dve.wait_ge(s_rpb, 16)
            link(dve.memset(toep, NEG))
            for v, (d0, d1) in enumerate(((0, 31), (7, 23))):
                for r in range(ROWS):
                    ins = dve.tensor_copy(toep[:, v, r, 16 + d0:16 + d1, :], rpbs[:, d0:d1, 7 - r:15 - r])
            ins.then_inc(s_toep, 1)
            ada_terms(0, 0)
            ada_rows(0, 0, 6)
            norm("m0")

            dve.wait_ge(s_yz, 16 * (2 + XTILES - 1))
            for u in range(1, 10, 2):
                dve.wait_ge(g_mm["win"], u + 1)
                dve.tensor_copy(lat[:, u % NT, u // NT * 336:(u // NT + 1) * 336], bank(5, 336)).then_inc(g_ed["win"], 1)
            dve.wait_ge(l_sd, 2)
            dve.reciprocal(st[:, 90:100], st[:, 90:100]).then_inc(l_rs, 1)
            dve.wait_ge(l_rs, 1)
            dve.wait_ge(s_par, 64)
            dve.wait_ge(g_ea["win"], 5)
            for t in range(NT):
                for (c0, c1), i in (((0, QL), 90), ((QL, QL + KVL), 95)):
                    dve.scalar_tensor_tensor(out=lat[:, t, c0:c1], in0=lat[:, t, c0:c1], scalar=st[:, i + t:i + t + 1],
                                             in1=latG[:, c0:c1], op0=ALU.mult, op1=ALU.mult).then_inc(l_n, 1)
            for t in range(6):
                dve.wait_ge(l_tr, t + 1)
                kt = (0, 1, 2, 3, 5, 4)[t]
                dve.tensor_copy(ckvT[:, :, kt * P:(kt + 1) * P], bank(2 * (t % 2) + 1, KVL).rearrange("p (c n) -> p c n", c=2)).then_inc(l_td, 1)
            dve.wait_ge(l_qr, 1)
            for u in range(1, 20, 2):
                dve.wait_ge(g_mm["uq"], u + 1)
                n, t = divmod(u, NT)
                dve.tensor_scalar(q[:, t, n * 384:(n + 1) * 384], bank(5, 384), MLA_SCALE, None, ALU.mult).then_inc(g_ed["uq"], 1)
            dve.wait_ge(s_toepd, 16 * 16)
            for u in range(1, 24, 2):
                dve.wait_ge(g_mm["uq"], 20 + u + 1)
                kt, n = divmod(u, 4)
                src = bank(5).rearrange("p (h c) -> p h c", h=4)
                dve.tensor_copy(kn[:, kt, n * 256:(n + 1) * 256].rearrange("p (h c) -> p h c", h=4), src[:, :, 0:NOPE])
                dve.tensor_copy(mv[:, kt, n * 256:(n + 1) * 256].rearrange("p (h c) -> p h c", h=4), src[:, :, NOPE:]).then_inc(g_ed["uq"], 1)

            def rinv(l, s):
                dve.wait_ge(a_ex, tiles_(l, s + 1))
                if s >= 4:
                    dve.wait_ge(a_o, tiles_(l, s - 3))
                dve.reciprocal(st[:, 108 + s % 4:109 + s % 4], st[:, 104 + s % 4:105 + s % 4]).then_inc(a_ri, 1)

            def pT_out(l, s, dst, src, n):
                dve.wait_ge(a_pt, tiles_(l, s + 1))
                if s >= 2:
                    dve.wait_ge(a_pv, tiles_(l, s - 1))
                dve.tensor_copy(dst[:, 0:n], src).then_inc(a_pe, 1)

            for s in range(NS + 1):
                if s < NS:
                    i = AT["S", s // NT, s % NT]
                    n = 640 if s % NT < CTX else P
                    dve.wait_ge(a_u[0], i + 1)
                    if s >= 4:
                        dve.wait_ge(a_ex, tiles_(0, s - 3))
                    dve.tensor_reduce(st[:, 100 + s % 4:101 + s % 4], bank(2 * (i % 2), n), AXX, ALU.max, negate=True).then_inc(a_mx, 1)
                if s >= 1:
                    n = 640 if (s - 1) % NT < CTX else P
                    rinv(0, s - 1)
                    pT_out(0, s - 1, PTm[(s - 1) % 2], bank(4, n), n)
                if s == 20:
                    ada_terms(0, 1)
                if s == 23:
                    ada_rows(0, 1, 7)
            ada_terms(1, 0)

            def out_projection(l):
                for c in range(1, KD, 2):
                    dve.wait_ge(o_tr, KD * l + c + 1)
                    dve.tensor_copy(OT[:, c, :], bank(2, 640)).then_inc(o_td, 1)
                name = f"wo{l}"
                dve.wait_ge(r_g, 32 * (2 * l + 1))
                for t in range(NT):
                    for j in range(2):
                        u = 2 * t + j
                        dve.wait_ge(g_mm[name], u + 1)
                        tt(tmpw[j], bank(4 + j), row(4 + t // CTX)[:, j * 512:(j + 1) * 512], ALU.mult).then_inc(g_ed[name], 1)
                        dve.wait_ge(g_ed[name], u + 1)
                        xs = x_(t)[:, j * 512:(j + 1) * 512]
                        ins = tt(xs, xs, tmpw[j], ALU.add)
                        if j == 1:
                            ins.then_inc(x_rdy, 1)

            def routing(l):
                def v3(at, n=80, t=NT):
                    return rt[:, at:at + n].rearrange("p (t e) -> p t e", t=t)

                sc, bi, ms, ky, tm = (v3(c) for c in (0, 80, 160, 240, 560))
                oh = [v3(320), v3(400)]
                M, pos = v3(480), v3(640)
                gg = [rt[:, 720 + 20 * i:740 + 20 * i].rearrange("p (t g) -> p t g", t=NT) for i in range(10)]
                sm = [rt[:, 920 + 5 * i:925 + 5 * i] for i in range(12)]
                cs, ext, pf, pg, base = (rt[:, 1000 + 16 * i:1016 + 16 * i] for i in range(5))
                tx, cmp_, pay = rt[0:1, 1100:1132], rt[0:1, 1140:1284], rt[:, 1290:1310]

                def over(v, n):
                    return v.unsqueeze(2).to_broadcast([P, NT, n])

                def iota(at, n):
                    return const[:, at:at + n].unsqueeze(1).to_broadcast([P, NT, n])

                def reduce(dst, src, op):
                    link(dve.tensor_reduce(dst, src, AXX, op))

                def first_max(dst, v, n, mx, kmin, key):
                    reduce(mx, v, ALU.max)
                    link(tt(key, v, over(mx, n), ALU.is_equal))
                    link(dve.scalar_tensor_tensor(out=key, in0=key, scalar=-64.0, in1=iota(C_I16, n), op0=ALU.mult, op1=ALU.add))
                    reduce(kmin, key, ALU.min)
                    link(tt(dst, key, over(kmin, n), ALU.is_equal))

                dve.wait_ge(rr_sg, l + 1)
                dve.wait_ge(s_par, 64)
                link(tt(bi, sc, rt[:, 1320:1336].unsqueeze(1).to_broadcast([P, NT, E]), ALU.add))
                b4 = rt[:, 80:160].rearrange("p (t g j) -> p t g j", t=NT, g=G4)
                b = [b4[:, :, :, j] for j in range(4)]
                link(tt(gg[0], b[0], b[1], ALU.max))
                link(tt(gg[1], b[0], b[1], ALU.min))
                link(tt(gg[2], b[2], b[3], ALU.max))
                link(tt(gg[3], b[2], b[3], ALU.min))
                link(tt(gg[4], gg[0], gg[2], ALU.max))
                link(tt(gg[5], gg[0], gg[2], ALU.min))
                link(tt(gg[6], gg[1], gg[3], ALU.max))
                link(tt(gg[5], gg[5], gg[6], ALU.max))
                link(tt(gg[4], gg[4], gg[5], ALU.add))
                first_max(gg[8], gg[4], G4, sm[0], sm[1], gg[7])
                gm = rt[:, 880:900].rearrange("p (t g) -> p t g", t=NT).unsqueeze(3).to_broadcast([P, NT, G4, 4])
                m4 = rt[:, 160:240].rearrange("p (t g j) -> p t g j", t=NT, g=G4)
                link(tt(m4, b4, gm, ALU.mult))
                link(dve.tensor_scalar(gg[9], gg[8], 1.0, -NEG, ALU.subtract, ALU.mult))
                g9 = rt[:, 900:920].rearrange("p (t g) -> p t g", t=NT).unsqueeze(3).to_broadcast([P, NT, G4, 4])
                link(tt(m4, m4, g9, ALU.add))
                for c in range(2):
                    first_max(oh[c], ms, E, sm[2], sm[3], ky)
                    if c == 0:
                        link(dve.scalar_tensor_tensor(out=ms, in0=oh[0], scalar=3 * NEG, in1=ms, op0=ALU.mult, op1=ALU.add))
                tt(M, oh[0], oh[1], ALU.add).then_inc(rr_m, 1)
                for c in range(2):
                    link(tt(tm, oh[c], sc, ALU.mult))
                    reduce(sm[4 + c], tm, ALU.add)
                link(tt(sm[6], sm[4], sm[5], ALU.add))
                link(dve.reciprocal(sm[7], sm[6]))
                p4 = pay.rearrange("p (t c w) -> p t c w", t=NT, c=2)
                pu = rt[:, 1290:1310].bitcast(U32).rearrange("p (t c w) -> p t c w", t=NT, c=2)
                for c in range(2):
                    link(tt(p4[:, :, c, 1], sm[4 + c], sm[7], ALU.mult))
                    link(dve.tensor_copy(pu[:, :, c, 0], const[:, C_TOK:C_TOK + NT]))
                dve.wait_ge(rr_cnt, l + 1)
                link(dve.tensor_copy(cs, bank(7, E, NT * E)))
                link(dve.tensor_copy(tm, bank(7, 80).rearrange("p (t e) -> p t e", t=NT)))
                link(dve.tensor_scalar(ext, cs, float(P), None, ALU.is_gt))
                for j in range(2, NT):
                    link(dve.scalar_tensor_tensor(out=ext, in0=cs, scalar=float(P * j), in1=ext, op0=ALU.is_gt, op1=ALU.add))
                src, dst = ext, pf
                for n in (1, 2, 4, 8):
                    link(dve.tensor_copy(dst[:, 0:n], src[:, 0:n]))
                    link(tt(dst[:, n:E], src[:, n:E], src[:, 0:E - n], ALU.add))
                    src, dst = dst, (pg if dst is pf else pf)
                incl = src
                link(tt(base, incl, ext, ALU.subtract))
                link(dve.tensor_scalar(base, base, float(P), float(P * (E - 1)), ALU.mult, ALU.add))
                e128 = const[:, C_E128:C_E128 + E]
                link(tt(base, base, e128, ALU.subtract))
                link(dve.tensor_scalar(ky, tm, float(P), None, ALU.is_ge))
                link(tt(ky, ky, base.unsqueeze(1).to_broadcast([P, NT, E]), ALU.mult))
                link(tt(ky, ky, tm, ALU.add))
                link(tt(pos, ky, iota(C_E128, E), ALU.add))
                ru = rti[:, :].rearrange("p (t c) -> p t c", c=2)
                for c in range(2):
                    link(tt(tm, oh[c], pos, ALU.mult))
                    reduce(sm[8 + c], tm, ALU.add)
                    link(dve.tensor_copy(ru[:, :, c], sm[8 + c]))
                dve.nop().then_inc(rr_pos, 1)
                link(dve.memset(tx, 0.0))
                link(dve.tensor_copy(tx[:, 0:E], const[0:1, C_I16:C_I16 + E]))
                cm = cmp_.rearrange("p (x e) -> p x e", x=XTILES)
                link(tt(cm, incl[0:1, :].unsqueeze(1).to_broadcast([1, XTILES, E]),
                        const[0:1, C_X9:C_X9 + XTILES].unsqueeze(2).to_broadcast([1, XTILES, E]), ALU.is_le))
                reduce(tx[:, E:MAXT], cm, ALU.add)
                link(dve.tensor_scalar(tx[:, E:MAXT], tx[:, E:MAXT], float(E - 1), None, ALU.min))
                link(dve.tensor_scalar(cmp_[:, 0:4], const[0:1, C_EVEN:C_EVEN + 4], incl[0:1, E - 1:E], None, ALU.is_le))
                reduce(cmp_[:, 4:5], cmp_[:, 0:4], ALU.add)
                link(dve.tensor_scalar(tx[:, 31:32], cmp_[:, 4:5], 8.0, None, ALU.add))
                dve.tensor_copy(rtx[:, :], tx).then_inc(rr_tab, 1)

            def moe(l):
                def rows_T(ready):
                    dve.wait_ge(e_tr[l], ready)
                    dve.tensor_copy(gatT[:, 4:8, :], bank(4).rearrange("p (c n) -> p c n", c=4)).then_inc(e_td[l], 1)

                def acts(par, ready, free):
                    dve.wait_ge(e_sg[l], ready)
                    tt(sig, sig, bank(0, DE), ALU.mult).then_inc(e_ga[l], 1)
                    dve.wait_ge(e_ga[l], ready)
                    if free is not None:
                        dve.wait_ge(e_at[l], free)
                    dve.scalar_tensor_tensor(out=actv, in0=sig, scalar=info[:, 2 * par + 1:2 * par + 2], in1=bank(0, DE, DE),
                                             op0=ALU.mult, op1=ALU.mult).then_inc(e_ac[l], 1)

                def acts_T(ready):
                    dve.wait_ge(e_at[l], ready)
                    dve.tensor_copy(actT, bank(5, DE).rearrange("p (c n) -> p c n", c=2)).then_inc(e_ae[l], 1)

                def y_out(ready, par, free):
                    dve.wait_ge(e_dn[l], ready)
                    dve.wait_ge(e_ys[l][par], free)
                    dve.tensor_copy(yb[par][:, 512:], bank(2)).then_inc(e_yd[l], 1)

                dve.nop().then_inc(e_yd[l], 1)
                rows_T(1)
                acts(0, 1, None)
                rows_T(2)
                acts_T(1)
                pairs = dve.value_load(rtx[0:1, 31:32], min_val=8, max_val=12)
                with dve.Fori(0, pairs) as i:
                    for j in range(2):
                        acts(1 - j, i * 2 + (2 + j), i * 2 + (1 + j))
                        rows_T(i * 2 + (3 + j))
                        y_out(i * 2 + (1 + j), j, i * 16 + 16)
                        acts_T(i * 2 + (2 + j))
                y_out(pairs * 2 + 1, 0, pairs * 16 + 16)

            def combine(l, nxt):
                dve.wait_ge(r_g, 32 * (2 * l + 2))
                for t in range(NT):
                    y0, y1 = cy[t % 2]
                    dve.wait_ge(c_in[l][t % 2], 32 * (t // 2 + 1))
                    link(tt(y0, y0, y1, ALU.add))
                    link(tt(y0, y0, row(4 + t // CTX), ALU.mult))
                    tt(x_(t), x_(t), y0, ALU.add).then_inc(x_rdy, 1)

            out_projection(0)
            ada_rows(1, 0, 7)
            norm("f0")
            routing(0)
            moe(0)
            combine(0, "m1")

            norm("m1")
            dve.wait_ge(kc_tr, 1)
            dve.tensor_copy(kcT[:, 4:8, :], bank(1).rearrange("p (c n) -> p c n", c=4)).then_inc(kc_td, 1)
            for u in range(1, 16, 2):
                dve.wait_ge(qk_mm, u + 1)
                if u < 8:
                    dve.tensor_scalar(qT[:, u, :], bank(0, 640), NAT_SCALE, None, ALU.mult).then_inc(qk_ed, 1)
                else:
                    dve.tensor_copy(kT[:, u - 8, :], bank(0, 640)).then_inc(qk_ed, 1)

            def v_out(u):
                dve.wait_ge(g_mm["vproj"], u + 1)
                j, t = divmod(u, NT)
                dve.tensor_copy(nv[:, t, j * 512:(j + 1) * 512], bank(5)).then_inc(g_ed["vproj"], 1)

            for u in (1, 3):
                v_out(u)
            dve.wait_ge(ko_tr, 1)
            dve.tensor_copy(kout[:, 512:], bank(1)).then_inc(ko_cd, 1)
            for u in (5, 7, 9):
                v_out(u)
            for s in range(NS + 2):
                if s < NS:
                    h, t = divmod(s, NT)
                    dve.wait_ge(a_u[1], s + 1)
                    if s >= 4:
                        dve.wait_ge(a_ex, tiles_(1, s - 3))
                    neg = st[:, 100 + s % 4:101 + s % 4]
                    if t < CTX:
                        if s >= 2:
                            dve.wait_ge(a_pt, tiles_(1, s - 1))
                        if t == 0:
                            dve.wait_ge(b_in[h % 2], 48 * (h // 2 + 1))
                            dve.wait_ge(b_ok, 2 * (h + 1))
                        mx = st[:, 112 + s % 4:113 + s % 4]
                        dve.tensor_tensor_reduce(out=Pn[s % 2], in0=bank(s % 4, 384), in1=biasb[h % 2][:, VARIANT[t], :], scale=1.0,
                                                 scalar=3 * NEG, op0=ALU.add, op1=ALU.max, accum_out=mx).then_inc(a_sx, 1)
                        dve.wait_ge(a_sx, 4 * h + t + 1)
                        dve.nop().then_inc(a_f[1], 1)
                        dve.tensor_scalar(neg, mx, -1.0, None, ALU.mult).then_inc(a_mx, 1)
                    else:
                        dve.tensor_reduce(neg, bank(s % 4, P), AXX, ALU.max, negate=True).then_inc(a_mx, 1)
                if s >= 1 and s - 1 < NS:
                    rinv(1, s - 1)
                    if (s - 1) % NT == CTX:
                        dve.nop().then_inc(a_f[1], 1)
                if s >= 2:
                    n = 384 if (s - 2) % NT < CTX else P
                    pT_out(1, s - 2, PTn[s % 2], bank(4 + s % 2, n), n)
            out_projection(1)
            norm("f1")
            routing(1)
            moe(1)
            combine(1, "fin")
            norm("fin")


def kernel(**inputs):
    import concourse.bacc as bacc
    from concourse.bass_utils import run_bass_kernel_spmd as run

    a = {n: np.asarray(v) for n, v in inputs.items()}

    def chunks(w, cols):
        k, n = w.shape
        v = w.reshape(k // P, P, n // cols, cols).transpose(2, 1, 0, 3)
        return np.ascontiguousarray(v).reshape(n // cols, P, -1)

    x = a["x_sample"][0].reshape(ROWS, GRID_W, D).transpose(1, 0, 2).reshape(-1, D)
    gu = np.stack([a["moe_w_gate"], a["moe_w_up"]], 3)
    gu = gu.reshape(DEPTH, E, KD, P, 2 * DE).transpose(0, 1, 3, 2, 4)
    down = a["moe_w_down"].reshape(DEPTH, E, 2, P, D).transpose(0, 1, 3, 2, 4)
    arrays = {
        "const": constants(),
        "x": np.concatenate([x, a["x_prompt"][0]], 0),
        "vecA": np.concatenate([a["b_ada"].reshape(96, P), a["c"].reshape(8, P), a["c_ctx"].reshape(8, P)], 0),
        "vecB": np.concatenate([a["norm_mix"].reshape(16, P), a["norm_ffn"].reshape(16, P)], 0),
        "ada": np.stack([chunks(w, 512) for w in a["w_ada"]], 0),
        "win": chunks(a["mla_w_in"][0], 336),
        "uq": chunks(a["mla_w_uq"][0], 768),
        "ukv": chunks(a["mla_w_ukv"][0], 2048)[0],
        "wo0": chunks(a["mla_w_o"][0], 512),
        "qkv": chunks(a["nat_w_qkv"][0], 512),
        "wo1": chunks(a["nat_w_o"][0], 512),
        "gu": gu.reshape(DEPTH, E, P, KD * 2 * DE),
        "down": down.reshape(DEPTH, E, P, 2 * D),
        "wr": a["w_router"].reshape(KD, P, E).transpose(1, 0, 2).reshape(P, KD * E),
        "rbias": a["router_bias"].reshape(1, E),
        "rpb": a["nat_rpb"][0].transpose(0, 2, 1).reshape(H, -1),
        "qnorm": a["mla_q_norm"].reshape(1, QL),
        "kvnorm": a["mla_kv_norm"].reshape(1, KVL),
        "gfin": a["norm_final"].reshape(1, D),
        "ckv": a["cache_mla_ckv"][0, 0],
        "krope": a["cache_mla_krope"][0, 0],
        "natk": a["cache_nat_k"][0, 0].reshape(P, D),
        "natv": a["cache_nat_v"][0, 0].reshape(P, D),
    }
    nc = bacc.Bacc("TRN2", target_bir_lowering=False, num_devices=1)
    arrays = {f"in_{n}": np.ascontiguousarray(v) for n, v in arrays.items()}
    ins = {n[3:]: nc.dram_tensor(n, v.shape, F32, kind="ExternalInput").ap() for n, v in arrays.items()}
    outs = {n: nc.dram_tensor(f"out_{n}", s, F32, kind="ExternalOutput").ap() for n, s in (
        ("y", (TOK, D)), ("ckv", (P, KVL)), ("krope", (P, ROPE)), ("k", (P, D)), ("v", (P, D)))}
    build(nc, ins, outs)
    r = run(nc, [arrays], core_ids=[0]).results[0]
    y = r["out_y"]
    ys = y[:512].reshape(GRID_W, ROWS, D).transpose(1, 0, 2).reshape(1, 512, D)
    return (y[512:].reshape(1, P, D), ys, r["out_ckv"].reshape(1, 1, P, KVL), r["out_krope"].reshape(1, 1, P, ROPE),
            r["out_k"].reshape(1, 1, P, H, 64), r["out_v"].reshape(1, 1, P, H, 64))
```

```python
from contextlib import ExitStack

import numpy as np

import concourse.bass as bass
from concourse import mybir

F32 = mybir.dt.float32
I32 = mybir.dt.int32
U32 = mybir.dt.uint32
ALU = mybir.AluOpType
ACT = mybir.ActivationFunctionType
AXX = mybir.AxisListType.X

P = 128
D = 1024
KD = D // P
NT = 5
CTX = 4
TOK = NT * P
DEPTH = 2
GRID_W, ROWS = 64, 8
H = 16
NOPE, ROPE, VD = 64, 32, 64
QD = NOPE + ROPE
QL, KVL = 384, 256
IN_DIM = QL + KVL + ROPE
MLA_SCALE = float(QD) ** -0.5
NAT_SCALE = 64.0 ** -0.5
E, G4, DE = 16, 4, 256
EPS = 1e-6
NEG = -1e30
LOCAL = 256
KEY0 = [0, 64, 192, 256]
VARIANT = [0, 1, 1, 2]
TOEP = 63
TSTART = [31, 23, 15]
TLEN = (TOEP - 15) * 8
XTILES = 9
MAXT = E + XTILES
SLOTS = (MAXT + 1) * P

NH = 768
MZ = 1340

C_ID, C_TRI, C_ONE = 0, 128, 256
C_MASK = 384
C_COS, C_SIN = 896, 960
C_TOK = 1024
C_I16 = 1032
C_E128 = 1048
C_X9 = 1064
C_EPS = 1073
C_EVEN = 1074
NCONST = 1078


def constants():
    c = np.zeros((P, NCONST), np.float32)
    p = np.arange(P)
    c[:, C_ID:C_ID + P] = np.eye(P)
    c[:, C_TRI:C_TRI + P] = p[:, None] < p[None, :]
    c[:, C_ONE:C_ONE + P] = 1.0
    qc, kc = p // ROWS, np.arange(LOCAL) // ROWS
    for n, (q0, k0) in enumerate(((0, 0), (48, 32))):
        q, k = q0 + qc[:, None], k0 + kc[None, :]
        start = np.clip(q - 8, 0, GRID_W - 16)
        c[:, C_MASK + n * LOCAL:C_MASK + (n + 1) * LOCAL] = np.where((k >= start) & (k < start + 16), 0.0, -NEG)
    inv = (10000.0 ** (-np.arange(8, dtype=np.float32) / 8)).astype(np.float32)
    for t in range(4):
        n = t * P + p
        ang = np.stack([(n % ROWS)[:, None] * inv, (n // ROWS)[:, None] * inv], 1).astype(np.float32)
        c[:, C_COS + 16 * t:C_COS + 16 * t + 16] = np.cos(ang).reshape(P, 16)
        c[:, C_SIN + 16 * t:C_SIN + 16 * t + 16] = np.sin(ang).reshape(P, 16)
    c[:, C_TOK:C_TOK + NT] = np.arange(NT)[None, :] * P + p[:, None]
    c[:, C_I16:C_I16 + E] = np.arange(E)
    c[:, C_E128:C_E128 + E] = np.arange(E) * P
    c[:, C_X9:C_X9 + XTILES] = np.arange(XTILES)
    c[:, C_EPS] = EPS
    c[:, C_EVEN:C_EVEN + 4] = [2, 4, 6, 8]
    return c


def build(nc, a, o):
    with ExitStack() as ctx:
        def sem(name):
            return ctx.enter_context(nc.semaphore(name))

        def sb(name, n, parts=P, dt=F32):
            return ctx.enter_context(nc.sbuf_tensor(name, [parts, n], dt))

        const = sb("const", NCONST)
        X = sb("resid", NT * D)
        W = sb("weights", 3 * 4096)
        HT = sb("ht", KD * TOK)
        R = sb("rows", 6 * D)
        BIG = sb("big", 20480)
        vecT = sb("vecT", 16)
        condT = sb("condT", 16)
        modrow = sb("modrow", 512)[0:2, :]
        latG = sb("latG", QL + KVL)
        st = sb("stats", 160)
        rt = sb("route", 1340 + 96)
        rti = sb("slot_of", 2 * NT, P, U32)
        rtx = sb("tiles", 32, 1, I32)
        wrt = sb("wrouter", KD * E)
        info = sb("info", 8)
        PS = ctx.enter_context(nc.psum_tensor("PS", [P, 8 * 512], F32))

        ident = const[:, C_ID:C_ID + P]
        ones = const[:, C_ONE:C_ONE + P]
        tri = const[:, C_TRI:C_TRI + P]

        def x_(t):
            return X[:, t * D:(t + 1) * D]

        def row(i):
            return R[:, i * D:(i + 1) * D]

        def w_(slot, k, n):
            return W[:, slot * 4096:slot * 4096 + k * n].rearrange("p (k n) -> p k n", k=k)

        def big(off, n, k=None):
            assert off + n <= 20480
            v = BIG[:, off:off + n]
            return v if k is None else v.rearrange("p (k n) -> p k n", k=k)

        def bank(b, n=512, at=0):
            return PS[:, b * 512 + at:b * 512 + at + n]

        hT = HT[:, :].rearrange("p (k t) -> p k t", k=KD)
        O = HT[:, :].rearrange("p (t n) -> p t n", t=NT)
        OT = big(0, 5120, KD)
        HB = [big(7296 + i * D, D) for i in range(NT)]
        tmpw = [big(13824 + i * 512, 512) for i in range(2)]
        lat = big(0, NT * IN_DIM, NT)
        q = big(0, 7680, NT)
        kn = big(7680, 6144, 6)
        mv = big(13824, 6144, 6)
        krw = big(19968, 192, 6)
        cqT = R[:, 0:1920].rearrange("p (k t) -> p k t", k=3)
        ckvT = R[:, 1920:3456].rearrange("p (k t) -> p k t", k=2)
        qTh = [R[:, i * 640:(i + 1) * 640] for i in range(2)]
        Pm = [R[:, 1280 + i * 640:1280 + (i + 1) * 640] for i in range(2)]
        PTm = [R[:, 2560 + i * 640:2560 + (i + 1) * 640] for i in range(2)]
        kTh = [R[:, 3840 + i * 768:3840 + (i + 1) * 768] for i in range(2)]
        ckc = R[:, 5376:5632]
        ropet = rt[:, 0:1024].rearrange("p (n h x i) -> p n h x i", n=4, h=H, x=2)
        qT = big(0, 5120, KD)
        kT = big(5120, 5120, KD)
        nv = big(10240, 5120, NT)
        nvs = big(15360, 3072, 3)
        kcr = big(15360, 1024)
        kout = big(16384, 1024)
        nvc = big(18432, 1024)
        kcT = big(19456, 1024, KD)
        biasb = [R[:, i * 1152:(i + 1) * 1152].rearrange("p (v k) -> p v k", v=3) for i in range(2)]
        qz = [rt[:, 0:TOK], latG[:, 0:TOK]]
        Pn = [R[:, 2304 + i * 384:2304 + (i + 1) * 384] for i in range(2)]
        PTn = [R[:, 3072 + i * 384:3072 + (i + 1) * 384] for i in range(2)]
        gat = HB[0:2]
        gatT = big(11776, D, KD)
        sig = big(12800, DE)
        actv = big(13056, DE)
        actT = big(13312, DE, 2)
        yb = [big(13568 + i * D, D) for i in range(2)]
        cy = [[big(t * D, D), big(14592 + t * D, D)] for t in range(NT)]
        vecs = big(7000, P)
        toep = BIG[0:H, 12416:12416 + 2 * ROWS * TOEP * ROWS].rearrange("h (v r d a) -> h v r d a", v=2, r=ROWS, a=ROWS)
        rpbs = BIG[0:H, 4500:4500 + 31 * 15].rearrange("h (d r) -> h d r", r=15)
        zero = big(3400, D)

        def ada_bias(i):
            return rt[0:2, 0:1024] if 6 <= i < 12 else BIG[0:2, 5632:6656]

        modD = nc.dram_tensor("modrows", [DEPTH, 2, 6 * D], F32).ap()
        toepD = nc.dram_tensor("toeplitz", [16, H, 2 * ROWS, TLEN], F32).ap()
        hD = [nc.dram_tensor(f"hrows{l}", [TOK, D], F32).ap() for l in range(DEPTH)]
        slotD = [nc.dram_tensor(f"slots{l}", [SLOTS, 2], F32).ap() for l in range(DEPTH)]
        yD = nc.dram_tensor("yrows", [MAXT * P, D], F32).ap()

        s_const, s_x, s_vec, s_par, s_ck = (sem(n) for n in ("const_in", "x_in", "vec_in", "gains_and_router_in", "mlacache_in"))
        s_yz, s_toep, s_toepd, s_rpb = (sem(n) for n in (
            "scratch_zeroed", "toep_built", "toep_stored", "rpb_in"))
        s_vt, s_vc, s_cond, s_sg = (sem(n) for n in ("vec_transposed", "vec_copied", "cond_ready", "cond_sigmoid"))
        s_dve, s_pool, s_act = sem("dve_chain"), sem("pool_chain"), sem("act_chain")
        NORMS = ("m0", "f0", "m1", "f1", "fin")
        n_sd, n_rs, n_ha, n_h, n_hd, n_tr, n_ta, n_td = (sem(f"norm_{n}") for n in (
            "sqrt", "rstd", "scaled", "h_pool", "h_dve", "transposed", "hT_act", "hT_dve"))
        n_st = sem("norm_stored")
        STORED = ("f0", "f1", "fin")

        def stored(norm):
            return 16 * NT * (STORED.index(norm) + 1)

        def upto(norm, tiles):
            return NORMS.index(norm) * NT + tiles

        x_rdy = sem("x_ready")
        r_ab = sem("rows_in")
        r_g = sem("gates_in")
        m_mm, m_b, m_cp, m_st = (sem(f"ada_{n}") for n in ("products", "bias_in", "rows", "stored"))
        w_in = [[sem(f"w{g}_in{i}") for i in range(3)] for g in range(2)]
        w_used = [sem(f"w{g}_used") for g in range(2)]
        g_mm, g_ed = ({n: sem(f"{n}_{x}") for n in ("win", "uq", "wo0", "vproj", "wo1")} for x in ("done", "taken_dve"))
        g_ea = {n: sem(f"{n}_taken_act") for n in ("win", "uq", "vproj")}
        l_sd, l_rs, l_n, l_tr, l_ta, l_td, l_rope, l_qr, k_rt, k_rc = (sem(n) for n in (
            "lat_sqrt", "lat_rstd", "lat_normed", "lat_transposed", "lat_T_act", "lat_T_dve",
            "k_rope_ready", "q_rope_ready", "krope_transposed", "krope_copied"))
        ATT = (0, 1)
        a_u, a_f = [sem(f"att{l}_unit_filled") for l in ATT], [sem("att0_unit_free")]
        a_mx, a_ex, a_ri, a_pt, a_pe, a_pv, a_o, o_tr, o_ta, o_td = (sem(f"att_{n}") for n in (
            "max", "exp", "rinv", "pT", "pT_sbuf", "pv", "o", "oT", "oT_act", "oT_dve"))

        def tiles_(l, n):
            return l * H * NT + n

        b_in = [sem(f"bias_in{i}") for i in range(2)]
        b_ok = sem("bias_masked")
        q_ok = sem("head_queries")
        qk_mm, qk_ea, qk_ed = sem("qkT_done"), sem("qkT_act"), sem("qkT_dve")
        kc_in, kc_tr, kc_ta, kc_td = sem("natcache_in"), sem("kcT_transposed"), sem("kcT_act"), sem("kcT_dve")
        ko_tr, ko_ca, ko_cd, ko_out = (sem(n) for n in ("kout_transposed", "kout_act", "kout_dve", "kout_stored"))
        vs_in = [sem(f"v_shifted{j}") for j in range(2)]
        rr_lg, rr_sg, rr_m, rr_cnt, rr_pos, rr_sc, rr_tab = (sem(n) for n in (
            "logits", "scores", "choice", "ranks", "positions", "slots_scattered", "tile_table"))
        e_gw, e_dw, e_inf, e_gt, e_gi, e_ys = ([[sem(f"moe{l}_{n}{i}") for i in range(2)] for l in range(DEPTH)] for n in (
            "gateup_in", "down_in", "tokens_in", "gates_in", "rows_in", "y_stored"))
        c_in = [sem(f"combine_in{t}") for t in range(NT)]
        c_sum = sem("combine_sum")
        (e_tr, e_ta, e_td, e_gu, e_sg, e_ga, e_ac, e_at, e_ae, e_dn, e_ya, e_yd) = (
            [sem(f"moe{l}_{n}") for l in range(DEPTH)] for n in (
                "rowsT", "rowsT_act", "rowsT_dve", "gateup", "sigmoid", "silu", "acts", "actsT", "actsT_sbuf",
                "down", "y_act", "y_dve"))
        e_end = sem("moe0_end")
        s_out = sem("outputs")
        e_gate = sem("gather_may_start")

        GAP_ADA = 11
        LOADS = [[("ada", 0, j) for j in range(4)] + [("win", 0, 0), ("win", 0, 1), ("ada", 0, 4), ("ada", 0, 5)]
                 + [("uq", 0, 0), ("uq", 0, 1), ("ukv", 0, 0)] + [("ada", 0, j) for j in range(6, 12)]
                 + [("wo0", 0, 0), ("wo0", 0, 1)] + [("ada", 1, j) for j in range(GAP_ADA)],
                 [("ada", 1, j) for j in range(GAP_ADA, 12)] + [("qkv", 0, j) for j in range(6)] + [("wo1", 0, 0), ("wo1", 0, 1)]]

        def ada_bank(i):
            return 6 + i % 2 if i < 6 else 7 if i < 12 else 4 + i % 2

        def source(what, l, j):
            return a["ada"][l, j] if what == "ada" else a["ukv"] if what == "ukv" else a[what][j]

        def w_wait(eng, what, l=0, j=0):
            g = 0 if (what, l, j) in LOADS[0] else 1
            n = LOADS[g].index((what, l, j))
            eng.wait_ge(w_in[g][ring(g, n)], 16 * (n // 3 + 1))
            return ring(g, n)

        def ring(g, n):
            return (n + g) % 3

        UNITS = [("K", 0), ("Q", 0)]
        for h in range(H):
            nxt = h + 1 < H
            UNITS += [("S", h, 0), ("S", h, 1)] + [("K", h + 1)] * nxt + [("S", h, 2)] + [("Q", h + 1)] * nxt
            UNITS += [("S", h, 3), ("S", h, 4)]
        AT = {u: i for i, u in enumerate(UNITS)}
        NS = H * NT

        block = ctx.enter_context(nc.Block())

        @block.sync
        def _(sp):
            sp.dma_start(const[:, :], a["const"]).then_inc(s_const, 16)
            sp.dma_start(vecs[0:16, :], a["cond"]).then_inc(s_vec, 16)

            def bias_in(i):
                sp.dma_start(ada_bias(i), a["adab"][i // 12, i % 12]).then_inc(m_b, 16)

            def ada_out(g, n):
                if not 0 <= n < len(LOADS[g]) or LOADS[g][n][0] != "ada":
                    return
                _, l, j = LOADS[g][n]
                i = l * 12 + j
                sp.wait_ge(m_cp, i + 1)
                sp.dma_start(modD[l, :, j * 512:(j + 1) * 512], modrow).then_inc(m_st, 16)
                if i + 1 == 6:
                    sp.wait_ge(l_qr, 2)
                if i + 1 == 12:
                    sp.wait_ge(o_tr, 1)
                if i + 1 < 24:
                    bias_in(i + 1)

            bias_in(0)

            def static_load(g, n):
                if n >= 3:
                    sp.wait_ge(w_used[g], n - 2)
                if (g, n) == (0, 6):
                    ada_out(g, 3)
                    sp.wait_ge(r_ab, 64)
                src = source(*LOADS[g][n])
                slot = ring(g, n)
                sp.dma_start(W[:, slot * 4096:slot * 4096 + src.shape[1]], src).then_inc(w_in[g][slot], 16)
                if (g, n) != (0, 6):
                    ada_out(g, n - 3)

            for n in range(len(LOADS[0])):
                static_load(0, n)
                if n == 7:
                    sp.wait_ge(s_toep, 1)
                    for qc in range(16):
                        sp.dma_start(toepD[qc], toep[:, :, :, 15 - qc:TOEP - qc, :].rearrange("h v r d a -> h (v r) (d a)")).then_inc(s_toepd, 16)
                if n == 3:
                    for t in range(NT):
                        sp.dma_start(x_(t), a["x"][t * P:(t + 1) * P, :]).then_inc(s_x, 16)

            for l in range(DEPTH):
                def load_gu(e, par):
                    sp.dma_start(W[:, par * 4096:(par + 1) * 4096], a["gu"][l][e]).then_inc(e_gw[l][par], 16)

                def load_dn(e, par):
                    at = 2 * 4096 + par * 2048
                    sp.dma_start(W[:, at:at + 2048], a["down"][l][e]).then_inc(e_dw[l][par], 16)

                last = len(LOADS[l]) - 3
                if l == 0:
                    for k in range(3):
                        sp.wait_ge(w_used[0], last + k + 1)
                        if ring(0, last + k) == 0:
                            load_gu(0, 0)
                        ada_out(0, last + k)
                    sp.wait_ge(e_gi[0][1], 16)
                    load_gu(1, 1)
                else:
                    for k in range(3):
                        sp.wait_ge(w_used[1], last + k + 1)
                        if ring(1, last + k) < 2:
                            load_gu(ring(1, last + k), ring(1, last + k))
                load_dn(0, 0)
                load_dn(1, 1)
                sp.wait_ge(e_gu[l], 1)
                load_gu(2, 0)
                sp.wait_ge(e_dn[l], 1)
                load_dn(2, 0)
                sp.wait_ge(rr_tab, l + 1)
                pairs = sp.value_load(rtx[0:1, 31:32], min_val=8, max_val=12)
                with sp.Fori(0, pairs - 1) as i:
                    for j in range(2):
                        e = sp.value_load(rtx[0:1, bass.ds(i * 2 + (3 + j), 1)], min_val=0, max_val=E - 1)
                        sp.wait_ge(e_gu[l], i * 2 + (2 + j))
                        load_gu(bass.ds(e, 1), 1 - j)
                        sp.wait_ge(e_dn[l], i * 2 + (2 + j))
                        load_dn(bass.ds(e, 1), 1 - j)
                if l == 0:
                    sp.wait_ge(e_gu[l], pairs * 2)
                    static_load(1, 0)
                    sp.wait_ge(e_end, 1)
                    sp.wait_ge(c_in[NT - 1], 32)
                    for n in range(1, len(LOADS[1])):
                        static_load(1, n)

            sp.wait_ge(s_out, 16 * 3)
            sp.wait_ge(ko_out, 16)

        @block.gpsimd
        def _(pool):
            chain = [0]

            def link(ins):
                chain[0] += 1
                ins.then_inc(s_pool, 1)
                pool.wait_ge(s_pool, chain[0])

            def spread(dst, l, cond, m, sm):
                pool.dma_start(dst, bass.AP(modD.tensor, ((l * 2 + cond) * 48 + m) * P, [[0, P], [1, D]])).then_inc(sm, 16)

            def rows_in(s, l, m):
                for c in range(2):
                    spread(row(c), l, c, m + 8, r_ab)
                    spread(row(2 + c), l, c, m, r_ab)

            def gates_in(s, l, m):
                for c in range(2):
                    spread(row(4 + c), l, c, m, r_g)

            def add_shift(s):
                for t in range(NT):
                    pool.wait_ge(n_ha, upto(s, t + 1))
                    pool.tensor_tensor(HB[t][:, 0:NH], HB[t][:, 0:NH], row(2 + t // CTX)[:, 0:NH], ALU.add).then_inc(n_h, 1)

            pool.dma_start(rpbs.rearrange("h d r -> h (d r)"), a["rpb"]).then_inc(s_rpb, 16)
            link(pool.memset(zero, 0.0))
            pool.dma_start(latG[:, 0:QL], bass.AP(a["qnorm"].tensor, 0, [[0, P], [1, QL]])).then_inc(s_par, 16)
            pool.dma_start(latG[:, QL:QL + KVL], bass.AP(a["kvnorm"].tensor, 0, [[0, P], [1, KVL]])).then_inc(s_par, 16)
            pool.dma_start(rt[:, 1320:1320 + E], bass.AP(a["rbias"].tensor, 0, [[0, P], [1, E]])).then_inc(s_par, 16)
            pool.dma_start(wrt[:, :], a["wr"]).then_inc(s_par, 16)
            pool.dma_start(ckc, a["ckv"]).then_inc(s_ck, 16)
            pool.wait_ge(m_st, 16 * 4)
            rows_in("m0", 0, 0)
            add_shift("m0")
            for l in range(DEPTH):
                pool.dma_start(slotD[l].rearrange("(p n) c -> p (n c)", p=P), zero[:, 0:SLOTS * 2 // P]).then_inc(s_yz, 16)
            for k in range(E + 1, MAXT):
                pool.dma_start(yD[k * P:(k + 1) * P, :], zero).then_inc(s_yz, 16)

            pool.wait_ge(s_toepd, 16 * 16)
            pool.dma_start(krw[:, 4, :], a["krope"]).then_inc(s_ck, 16)
            pool.wait_ge(g_ea["win"], 5)
            pool.wait_ge(g_ed["win"], 5)
            pool.dma_start(o["krope"], lat[:, CTX, QL + KVL:IN_DIM]).then_inc(s_out, 16)

            def rotate(src, dst, t, nh):
                cs, sn = (const[:, c + 16 * t:c + 16 * t + 16].rearrange("p (x i) -> p x i", x=2).unsqueeze(1).to_broadcast([P, nh, 2, 8])
                          for c in (C_COS, C_SIN))
                tm = [ropet[:, n, 0:nh] for n in range(4)]
                x1, x2 = src[:, :, :, 0, :], src[:, :, :, 1, :]
                link(pool.tensor_tensor(tm[0], x1, cs, ALU.mult))
                link(pool.tensor_tensor(tm[1], x2, sn, ALU.mult))
                link(pool.tensor_tensor(tm[2], x1, sn, ALU.mult))
                link(pool.tensor_tensor(tm[3], x2, cs, ALU.mult))
                link(pool.tensor_tensor(dst[:, :, :, 0, :], tm[0], tm[1], ALU.subtract))
                return pool.tensor_tensor(dst[:, :, :, 1, :], tm[2], tm[3], ALU.add)

            def halves(v, nh):
                return v.rearrange("p (h x f i) -> p h x f i", h=nh, x=2, f=2)

            for t in range(4):
                link(rotate(halves(lat[:, t, QL + KVL:IN_DIM], 1), halves(krw[:, t, :], 1), t, 1))
            pool.tensor_copy(krw[:, 5, :], lat[:, CTX, QL + KVL:IN_DIM]).then_inc(l_rope, 1)
            pool.wait_ge(l_n, 10)
            pool.dma_start(o["ckv"], lat[:, CTX, QL:QL + KVL]).then_inc(s_out, 16)
            pool.wait_ge(s_out, 32)
            pool.nop().then_inc(l_qr, 1)
            pool.wait_ge(g_ea["uq"], 10)
            pool.wait_ge(g_ed["uq"], 10)
            for t in range(4):
                v = q[:, t, :].rearrange("p (h n) -> p h n", h=H)[:, :, NOPE:QD].rearrange("p h (x f i) -> p h x f i", x=2, f=2)
                link(rotate(v, v, t, H))
            pool.nop().then_inc(l_qr, 1)

            def combine_gathers(l):
                for t in range(NT):
                    for c in range(2):
                        n = 2 * t + c
                        pool.indirect_dma_start(cy[t][c], None, yD, bass.IndirectOffsetOnAxis(ap=rti[:, n:n + 1], axis=0)).then_inc(c_in[t], 16)
                for t in range(2, NT):
                    pool.wait_ge(c_in[t], 32 * (l + 1))
                    pool.tensor_tensor(cy[t][0], cy[t][0], cy[t][1], ALU.add).then_inc(c_sum, 1)

            def attention_1():
                add_shift("m1")
                pool.wait_ge(x_rdy, upto("m1", NT) - NT)
                pool.dma_start(kcr, a["natk"]).then_inc(kc_in, 16)
                pool.dma_start(nvc, a["natv"]).then_inc(kc_in, 16)
                gates_in("m1", 1, 16)
                pool.wait_ge(n_h, upto("m1", NT))
                pool.wait_ge(n_hd, upto("m1", NT))
                for i in range(2):
                    link(pool.memset(biasb[i][:, :, LOCAL:], 0.0))
                    link(pool.memset(qz[i][64 - 64 * i:128 - 64 * i, :], 0.0))
                pool.wait_ge(s_toepd, 16 * 16)

                def bias_tiles(h):
                    b = biasb[h % 2]
                    if h >= 2:
                        pool.wait_ge(a_mx, tiles_(1, NT * (h - 1)))
                    for v in range(3):
                        off = (h * 2 + (v == 1)) * ROWS * TLEN + (TSTART[v] - 15) * ROWS
                        src = bass.AP(toepD.tensor, off, [[H * 2 * ROWS * TLEN, 16], [TLEN, ROWS], [1, LOCAL]])
                        pool.dma_start(b[:, v, 0:LOCAL], src).then_inc(b_in[h % 2], 16)
                    pool.wait_ge(b_in[h % 2], 48 * (h // 2 + 1))
                    for n, v in enumerate((0, 2)):
                        mask = const[:, C_MASK + n * LOCAL:C_MASK + (n + 1) * LOCAL]
                        pool.tensor_tensor(b[:, v, 0:LOCAL], b[:, v, 0:LOCAL], mask, ALU.add).then_inc(b_ok, 1)

                for h in range(2):
                    bias_tiles(h)
                pool.wait_ge(ko_ca, 1)
                pool.wait_ge(ko_cd, 1)
                pool.dma_start(o["k"], kout).then_inc(ko_out, 16)
                pool.wait_ge(ko_out, 16)
                for j in range(2):
                    pool.wait_ge(g_ea["vproj"], (3, 5)[j])
                    pool.wait_ge(g_ed["vproj"], (2, 5)[j])
                    cols = slice(j * 512, (j + 1) * 512)
                    for i in range(3):
                        pool.dma_start(nvs[0:64, i, cols], nv[64:128, i, cols]).then_inc(vs_in[j], 16)
                        pool.dma_start(nvs[64:128, i, cols], nv[0:64, i + 1, cols]).then_inc(vs_in[j], 16)
                pool.dma_start(o["v"], nv[:, CTX, :]).then_inc(s_out, 16)
                for h in range(2, H):
                    bias_tiles(h)

            pay = rt[:, 1290:1310]
            for l in range(DEPTH):
                if l == 1:
                    attention_1()
                s = f"f{l}"
                pool.wait_ge(o_tr, KD * l + KD)
                pool.wait_ge(m_st, 16 * 12 * (l + 1))
                if l == 0:
                    gates_in("m0", 0, 16)
                rows_in(s, l, 24)
                add_shift(s)
                pool.wait_ge(x_rdy, upto(s, NT) - NT)
                gates_in(s, l, 40)
                pool.wait_ge(n_st, stored(s))
                pool.wait_ge(s_yz, 16 * (2 + XTILES - 1))
                pool.wait_ge(rr_pos, l + 1)
                for t in range(NT):
                    for c in range(2):
                        n = 2 * t + c
                        pool.indirect_dma_start(slotD[l], bass.IndirectOffsetOnAxis(ap=rti[:, n:n + 1], axis=0),
                                                pay[:, 2 * n:2 * n + 2], None).then_inc(rr_sc, 16)
                pool.wait_ge(rr_sc, 160 * (l + 1))
                pool.wait_ge(rr_tab, l + 1)
                pairs = pool.value_load(rtx[0:1, 31:32], min_val=8, max_val=12)

                def tokens_in(rows, par):
                    pool.dma_start(info[:, 2 * par:2 * par + 2], slotD[l][rows, :]).then_inc(e_inf[l][par], 16)

                def gates_of(rows, par):
                    pool.dma_start(info[:, 4 + 2 * par:6 + 2 * par], slotD[l][rows, :]).then_inc(e_gt[l][par], 16)

                def rows_of(par):
                    pool.indirect_dma_start(gat[par], None, hD[l], bass.IndirectOffsetOnAxis(
                        ap=info[:, 2 * par:2 * par + 1].bitcast(U32), axis=0)).then_inc(e_gi[l][par], 16)

                for k in range(2):
                    tokens_in(slice(k * P, (k + 1) * P), k)
                for k in range(2):
                    pool.wait_ge(e_inf[l][k], 16)
                    rows_of(k)
                for k in range(2):
                    gates_of(slice(k * P, (k + 1) * P), k)
                if l == 1:
                    pool.wait_ge(n_h, upto("f1", NT))
                    pool.wait_ge(n_hd, upto("f1", NT))
                    pool.dma_start(row(0), bass.AP(a["gfin"].tensor, 0, [[0, P], [1, D]])).then_inc(r_ab, 16)
                with pool.Fori(0, pairs) as i:
                    for j in range(2):
                        rows = bass.ds(i * (2 * P) + (2 + j) * P, P)
                        pool.wait_ge(e_gi[l][j], i * 16 + 16)
                        pool.nop().then_inc(e_gate, 1)
                        tokens_in(rows, j)
                        pool.wait_ge(e_inf[l][j], i * 16 + 32)
                        pool.wait_ge(e_tr[l], i * 2 + (1 + j))
                        pool.nop().then_inc(e_gate, 1)
                        rows_of(j)
                        pool.wait_ge(e_ac[l], i * 2 + (1 + j))
                        pool.nop().then_inc(e_gate, 1)
                        gates_of(rows, j)
                if l == 0:
                    pool.wait_ge(m_st, 16 * 16)
                    rows_in("m1", 1, 0)
                pool.wait_ge(e_ys[l][0], pairs * 16 + 32)
                pool.wait_ge(e_ys[l][1], pairs * 16 + 16)
                pool.nop().then_inc(e_gate, 1)
                combine_gathers(l)

        @block.tensor
        def _(pe):
            def transpose(dst, src, n=P):
                return pe.transpose(dst, src, const[0:n, C_ID:C_ID + n])

            def ada(l, j):
                i = l * 12 + j
                one = 6 <= i < 12
                if j >= 2 or i == 12:
                    pe.wait_ge(m_cp, i - (0 if one else 1))
                w = w_(w_wait(pe, "ada", l, j), KD, 512)
                for k in range(KD):
                    ins = pe.matmul(PS[0:2, ada_bank(i) * 512:ada_bank(i) * 512 + 512], condT[:, 2 * k:2 * k + 2], w[:, k, :],
                                    start=(k == 0), stop=(k == KD - 1))
                ins.then_inc(m_mm, 1)
                pe.wait_ge(m_mm, i + 1)
                pe.nop().then_inc(w_used[0 if ("ada", l, j) in LOADS[0] else 1], 1)

            def norm_transposes(s):
                for t in range(NT + 1):
                    if t < NT:
                        if s == "f0":
                            ada(1, t)
                        pe.wait_ge(n_h, upto(s, t + 1))
                        pe.wait_ge(n_hd, upto(s, t + 1))
                        if t >= 2:
                            pe.wait_ge(n_ta, upto(s, t - 1))
                            pe.wait_ge(n_td, upto(s, t - 1))
                        for c in range(KD):
                            ins = transpose(bank(2 * (t % 2), P, c * P), HB[t][:, c * P:(c + 1) * P])
                        ins.then_inc(n_tr, 1)
                    if t >= 1 and s[0] == "f":
                        pe.wait_ge(n_ta, upto(s, t))
                        pe.wait_ge(n_td, upto(s, t))
                        if t == 1:
                            pe.wait_ge(s_par, 64)
                        for k in range(KD):
                            ins = pe.matmul(bank(6, E, (t - 1) * E), hT[:, k, (t - 1) * P:t * P], wrt[:, k * E:(k + 1) * E],
                                            start=(k == 0), stop=(k == KD - 1))
                        ins.then_inc(rr_lg, 1)

            def gemm_unit(name, u, n, ks, lhs, rhs, done=None):
                if u >= 2:
                    pe.wait_ge(g_ea[name] if u % 2 == 0 else g_ed[name], u // 2)
                for k in range(ks):
                    ins = pe.matmul(bank(4 + u % 2, n), lhs(k), rhs(k), start=(k == 0), stop=(k == ks - 1))
                ins.then_inc(g_mm[name], 1)

            pe.wait_ge(s_const, 16)
            pe.wait_ge(s_vec, 16)
            pe.transpose(bank(6, 16), vecs[0:16, :], const[0:16, C_ID:C_ID + 16]).then_inc(s_vt, 1)
            pe.wait_ge(s_cond, 1)
            for j in range(4):
                ada(0, j)
            norm_transposes("m0")

            pe.wait_ge(n_ta, upto("m0", NT))
            pe.wait_ge(n_td, upto("m0", NT))
            for j in range(2):
                w = w_(w_wait(pe, "win", 0, j), KD, 336)
                for t in range(NT):
                    gemm_unit("win", j * NT + t, 336, KD, lambda k: hT[:, k, t * P:(t + 1) * P], lambda k: w[:, k, :])
                pe.wait_ge(g_mm["win"], (j + 1) * NT)
                pe.nop().then_inc(w_used[0], 1)
            ada(0, 4)
            ada(0, 5)
            pe.wait_ge(s_ck, 32)
            for t in range(6):
                if t < NT:
                    pe.wait_ge(l_n, 2 * t + 2)
                if t >= 2:
                    pe.wait_ge(l_ta, t - 1)
                    pe.wait_ge(l_td, t - 1)
                b = 2 * (t % 2)
                if t < NT:
                    for c in range(3):
                        transpose(bank(b, P, c * P), lat[:, t, c * P:(c + 1) * P])
                for c in range(2):
                    src = lat[:, t, QL + c * P:QL + (c + 1) * P] if t < NT else ckc[:, c * P:(c + 1) * P]
                    ins = transpose(bank(b + 1, P, c * P), src)
                ins.then_inc(l_tr, 1)
            pe.wait_ge(l_rope, 1)
            pe.wait_ge(l_ta, 5)
            pe.wait_ge(l_td, 6)
            for kt in range(6):
                ins = transpose(PS[0:ROPE, kt * P:(kt + 1) * P], krw[:, kt, :])
            ins.then_inc(k_rt, 1)
            for j in range(2):
                w = w_(w_wait(pe, "uq", 0, j), 3, 768)
                for n in range(2):
                    for t in range(NT):
                        gemm_unit("uq", (j * 2 + n) * NT + t, 384, 3, lambda k: cqT[:, k, t * P:(t + 1) * P],
                                  lambda k: w[:, k, n * 384:(n + 1) * 384])
                pe.wait_ge(g_mm["uq"], (j + 1) * 10)
                pe.nop().then_inc(w_used[0], 1)
            w = w_(w_wait(pe, "ukv"), 2, 2048)
            for kt in range(6):
                for n in range(4):
                    gemm_unit("uq", 20 + kt * 4 + n, 512, 2, lambda k: ckvT[:, k, kt * P:(kt + 1) * P],
                              lambda k: w[:, k, n * 512:(n + 1) * 512])
            pe.wait_ge(g_mm["uq"], 44)
            pe.nop().then_inc(w_used[0], 1)

            def mla_pT(s):
                pe.wait_ge(a_ex, tiles_(0, s + 1))
                if s >= 1:
                    pe.wait_ge(a_pe, tiles_(0, s))
                n = NT if s % NT < CTX else 1
                for c in range(n):
                    ins = transpose(bank(4, P, c * P), Pm[s % 2][:, c * P:(c + 1) * P])
                ins.then_inc(a_pt, 1)

            def mla_pv(s):
                h, t = divmod(s, NT)
                pe.wait_ge(a_pe, tiles_(0, s + 1))
                if s >= 1:
                    pe.wait_ge(a_o, tiles_(0, s))
                tiles = list(range(5)) if t < CTX else [5]
                for c, kt in enumerate(tiles):
                    ins = pe.matmul(bank(6, VD), PTm[s % 2][:, c * P:(c + 1) * P], mv[:, kt, h * VD:(h + 1) * VD],
                                    start=(c == 0), stop=(c == len(tiles) - 1))
                ins.then_inc(a_pv, 1)

            pe.wait_ge(k_rc, 1)
            pe.wait_ge(g_ea["uq"], 22)
            pe.wait_ge(g_ed["uq"], 22)
            pe.wait_ge(l_qr, 2)
            for i, u in enumerate(UNITS):
                b = 2 * (i % 2)
                if i >= 2:
                    pe.wait_ge(a_f[0], i - 1)
                h = u[1]
                if u[0] == "K":
                    for kt in range(6):
                        ins = transpose(PS[0:NOPE, b * 512 + kt * P:b * 512 + (kt + 1) * P], kn[:, kt, h * NOPE:(h + 1) * NOPE])
                    ins.then_inc(a_u[0], 1)
                elif u[0] == "Q":
                    for t in range(NT):
                        ins = transpose(PS[0:QD, b * 512 + t * P:b * 512 + (t + 1) * P], q[:, t, h * QD:(h + 1) * QD])
                    ins.then_inc(a_u[0], 1)
                else:
                    t, s = u[2], h * NT + u[2]
                    if t == 0:
                        pe.wait_ge(a_f[0], max(AT["Q", h], AT["K", h]) + 1)
                    lhs = qTh[h % 2][0:QD, t * P:(t + 1) * P]
                    if t < CTX:
                        pe.matmul(bank(b), lhs, kTh[h % 2][0:QD, 0:512], start=True, stop=True)
                        ins = pe.matmul(bank(b + 1, P), lhs, kTh[h % 2][0:QD, 512:640], start=True, stop=True)
                    else:
                        ins = pe.matmul(bank(b, P), lhs, kTh[h % 2][0:QD, 640:768], start=True, stop=True)
                    ins.then_inc(a_u[0], 1)
                    if s >= 1:
                        mla_pT(s - 1)
                    if s >= 2:
                        mla_pv(s - 2)
                    if t == CTX and h < 6:
                        ada(0, 6 + h)
            mla_pT(NS - 1)
            mla_pv(NS - 2)
            mla_pv(NS - 1)

            def out_projection(l):
                for c in range(KD):
                    if c == 0:
                        pe.wait_ge(a_o, tiles_(l, NS))
                    if c >= 2:
                        pe.wait_ge(o_td if c % 2 else o_ta, 4 * l + c // 2)
                    b = 2 * (c % 2)
                    for t in range(NT):
                        ins = transpose(bank(b, P, t * P), O[:, t, c * P:(c + 1) * P])
                    ins.then_inc(o_tr, 1)
                name = f"wo{l}"
                w = [w_(w_wait(pe, name, 0, j), KD, 512) for j in range(2)]
                pe.wait_ge(o_ta, 4 * l + 4)
                pe.wait_ge(o_td, 4 * l + 4)
                for t in range(NT):
                    for j in range(2):
                        u = 2 * t + j
                        if u >= 2:
                            pe.wait_ge(g_ed[name], u - 1)
                        for k in range(KD):
                            ins = pe.matmul(bank(4 + j), OT[:, k, t * P:(t + 1) * P], w[j][:, k, :], start=(k == 0), stop=(k == KD - 1))
                        ins.then_inc(g_mm[name], 1)
                pe.wait_ge(g_mm[name], 2 * NT)
                pe.nop().then_inc(w_used[l], 2)

            def routing(l):
                pe.wait_ge(rr_m, l + 1)
                M = rt[:, MZ:MZ + 96]
                pe.matmul(bank(7, 96), ones, M, start=True, stop=False)
                for n in range(2, NT + 1):
                    pe.matmul(bank(7, 96 - n * E, n * E), ones, M[:, E:96 - (n - 1) * E], start=False, stop=False)
                ins = pe.matmul(bank(7, 80), tri, M[:, E:96], start=False, stop=True)
                ins.then_inc(rr_cnt, 1)

            def moe(l):
                pairs = None

                def rows_T(par, gi):
                    pe.wait_ge(e_gi[l][par], gi)
                    for c in range(KD):
                        ins = transpose(bank(3, P, c * P), gat[par][:, c * P:(c + 1) * P])
                    ins.then_inc(e_tr[l], 1)

                def gateup(par, w_ready, rows_ready):
                    pe.wait_ge(e_gw[l][par], w_ready)
                    pe.wait_ge(e_ta[l], rows_ready)
                    pe.wait_ge(e_td[l], rows_ready)
                    w = w_(par, KD, 512)
                    for k in range(KD):
                        ins = pe.matmul(bank(0), gatT[:, k, :], w[:, k, :], start=(k == 0), stop=(k == KD - 1))
                    ins.then_inc(e_gu[l], 1)

                def acts_T(ready):
                    pe.wait_ge(e_ac[l], ready)
                    for c in range(2):
                        ins = transpose(bank(5, P, c * P), actv[:, c * P:(c + 1) * P])
                    ins.then_inc(e_at[l], 1)

                def down(par, w_ready, acts_ready, free):
                    pe.wait_ge(e_dw[l][par], w_ready)
                    pe.wait_ge(e_ae[l], acts_ready)
                    pe.wait_ge(e_ya[l], free)
                    pe.wait_ge(e_yd[l], free)
                    w = W[:, 8192 + par * 2048:8192 + (par + 1) * 2048].rearrange("p (k n) -> p k n", k=2)
                    for n in range(2):
                        for k in range(2):
                            ins = pe.matmul(bank(1 + n), actT[:, k, :], w[:, k, n * 512:(n + 1) * 512], start=(k == 0), stop=(k == 1))
                    ins.then_inc(e_dn[l], 1)

                rows_T(0, 16)
                gateup(0, 16, 1)
                rows_T(1, 16)
                acts_T(1)
                pe.wait_ge(rr_tab, l + 1)
                pairs = pe.value_load(rtx[0:1, 31:32], min_val=8, max_val=12)
                with pe.Fori(0, pairs) as i:
                    for j in range(2):
                        par = 1 - j
                        gateup(par, i * 16 + 16 * (1 + j), i * 2 + (2 + j))
                        rows_T(j, i * 16 + 32)
                        down(1 - par, i * 16 + 16, i * 2 + (1 + j), i * 2 + (1 + j))
                        acts_T(i * 2 + (2 + j))
                down(0, pairs * 16 + 16, pairs * 2 + 1, pairs * 2 + 1)
                pe.wait_ge(e_dn[l], pairs * 2 + 1)
                pe.wait_ge(e_ta[l], pairs * 2 + 2)
                pe.wait_ge(e_td[l], pairs * 2 + 2)
                if l == 0:
                    pe.nop().then_inc(e_end, 1)

            out_projection(0)
            pe.wait_ge(g_ed["wo0"], 2 * NT)
            norm_transposes("f0")
            ada(1, NT)
            ada(1, NT + 1)
            routing(0)
            for j in range(NT + 2, GAP_ADA):
                ada(1, j)
            pe.wait_ge(m_cp, 12 + GAP_ADA)
            moe(0)
            for j in range(GAP_ADA, 12):
                ada(1, j)

            norm_transposes("m1")
            pe.wait_ge(kc_in, 32)
            pe.wait_ge(n_ta, upto("m1", NT))
            pe.wait_ge(n_td, upto("m1", NT))
            for c in range(KD):
                ins = transpose(bank(0, P, c * P), kcr[:, c * P:(c + 1) * P])
            ins.then_inc(kc_tr, 1)
            for u in range(16):
                if u % 4 == 0:
                    w = w_(w_wait(pe, "qkv", 0, u // 4), KD, 512)
                if u == 1:
                    pe.wait_ge(kc_ta, 1)
                    pe.wait_ge(kc_td, 1)
                if u >= 2:
                    pe.wait_ge(qk_ea if u % 2 == 0 else qk_ed, u // 2)
                b = (2, 0)[u % 2]
                m = u % 4
                for n0, n1, bb in ((0, 512, b), (512, 640, b + 1)):
                    for k in range(KD):
                        ins = pe.matmul(bank(bb, n1 - n0), w[:, k, m * P:(m + 1) * P], hT[:, k, n0:n1], start=(k == 0), stop=(k == KD - 1))
                ins.then_inc(qk_mm, 1)
                if u % 4 == 3:
                    pe.wait_ge(qk_mm, u + 1)
                    pe.nop().then_inc(w_used[1], 1)
            for j in range(2):
                w = w_(w_wait(pe, "qkv", 0, 4 + j), KD, 512)
                for t in range(NT):
                    gemm_unit("vproj", j * NT + t, 512, KD, lambda k: hT[:, k, t * P:(t + 1) * P], lambda k: w[:, k, :])
                    if (j, t) == (0, 1):
                        pe.wait_ge(qk_ea, 8)
                        pe.wait_ge(qk_ed, 8)
                        for c in range(KD):
                            ins = transpose(bank(0, P, c * P), kT[:, c, 512:640])
                        ins.then_inc(ko_tr, 1)
                pe.wait_ge(g_mm["vproj"], (j + 1) * NT)
                pe.nop().then_inc(w_used[1], 1)

            def nat_scores(s):
                h, t = divmod(s, NT)
                if s >= 4:
                    pe.wait_ge(a_mx, tiles_(1, s - 3))
                    pe.wait_ge(a_ex, tiles_(1, s - 3))
                hp = h // 2
                lhs = qz[h % 2][:, t * P:(t + 1) * P]
                if t == 0:
                    pe.wait_ge(q_ok, h + 1)
                    pe.wait_ge(b_ok, 2)
                if t < CTX:
                    pe.matmul(bank(s % 4, LOCAL), lhs, kT[:, hp, KEY0[t]:KEY0[t] + LOCAL], start=True, stop=True)
                    ins = pe.matmul(bank(s % 4, P, LOCAL), lhs, kcT[:, hp, :], start=True, stop=True)
                else:
                    ins = pe.matmul(bank(s % 4, P), lhs, kT[:, hp, 512:640], start=True, stop=True)
                ins.then_inc(a_u[1], 1)

            def nat_pT(s):
                pe.wait_ge(a_ex, tiles_(1, s + 1))
                if s >= 2:
                    pe.wait_ge(a_pe, tiles_(1, s - 1))
                for c in range(3 if s % NT < CTX else 1):
                    ins = transpose(bank(4 + s % 2, P, c * P), Pn[s % 2][:, c * P:(c + 1) * P])
                ins.then_inc(a_pt, 1)

            def nat_pv(s):
                h, t = divmod(s, NT)
                pe.wait_ge(a_pe, tiles_(1, s + 1))
                if s >= 2:
                    pe.wait_ge(a_o, tiles_(1, s - 1))
                cols = slice(h * VD, (h + 1) * VD)
                cache = nvc[:, cols]
                vals = [[nv[:, 0, cols], nv[:, 1, cols], cache], [nvs[:, 0, cols], nvs[:, 1, cols], cache],
                        [nvs[:, 1, cols], nvs[:, 2, cols], cache], [nv[:, 2, cols], nv[:, 3, cols], cache], [nv[:, 4, cols]]][t]
                for c, v in enumerate(vals):
                    ins = pe.matmul(bank(6 + s % 2, VD), PTn[s % 2][:, c * P:(c + 1) * P], v, start=(c == 0), stop=(c == len(vals) - 1))
                ins.then_inc(a_pv, 1)

            pe.wait_ge(ko_ca, 1)
            pe.wait_ge(ko_cd, 1)
            pe.wait_ge(g_ea["vproj"], 5)
            pe.wait_ge(g_ed["vproj"], 5)
            for s in range(NS + 3):
                if s < NS:
                    nat_scores(s)
                if s in (3, 3 + NS // 2):
                    pe.wait_ge(vs_in[s // (NS // 2)], 96)
                if 2 <= s < NS + 2:
                    nat_pT(s - 2)
                if s >= 3:
                    nat_pv(s - 3)
            out_projection(1)
            norm_transposes("f1")
            routing(1)
            moe(1)

        @block.scalar
        def _(act):
            chain = [0]

            def link(ins):
                chain[0] += 1
                ins.then_inc(s_act, 1)
                act.wait_ge(s_act, chain[0])

            def norm(s):
                i = NORMS.index(s)
                ss, sd = (st[:, n + 5 * i:n + 5 * i + 5] for n in (0, 25))
                lag = NT if s[0] == "f" and s != "fin" else 2
                for t in range(NT + lag):
                    if t < NT:
                        if s == "m0":
                            act.wait_ge(s_x, 16 * NT)
                        else:
                            act.wait_ge(x_rdy, upto(s, t + 1) - NT)
                        link(act.activation(HB[t], x_(t), ACT.Square, accum_out=ss[:, t:t + 1]))
                        act.activation(sd[:, t:t + 1], ss[:, t:t + 1], ACT.Sqrt, scale=1.0 / D, bias=const[:, C_EPS:C_EPS + 1]).then_inc(n_sd, 1)
                    if t >= lag:
                        v = t - lag
                        rows = slice(v * P, (v + 1) * P)
                        if s == "fin":
                            act.wait_ge(n_ha, upto(s, v + 1))
                            act.dma_start(o["y"][rows, :], HB[v]).then_inc(n_st, 16)
                            continue
                        act.wait_ge(n_tr, upto(s, v + 1))
                        act.activation(hT[:, 0:4, rows], bank(2 * (v % 2)).rearrange("p (c n) -> p c n", c=4), ACT.Copy).then_inc(n_ta, 1)
                        if s[0] == "f":
                            act.dma_start(hD[int(s[1])][rows, :], HB[v]).then_inc(n_st, 16)
                if s == "fin":
                    act.wait_ge(n_st, stored(s))

            act.wait_ge(s_vc, 1)
            act.activation(st[:, 144:160], vecT[:, 0:16], ACT.Sigmoid).then_inc(s_sg, 1)
            act.wait_ge(s_const, 16)
            norm("m0")

            for u in range(0, 10, 2):
                act.wait_ge(g_mm["win"], u + 1)
                act.activation(lat[:, u % NT, u // NT * 336:(u // NT + 1) * 336], bank(4, 336), ACT.Copy).then_inc(g_ea["win"], 1)
            act.wait_ge(g_ea["win"], 5)
            act.wait_ge(g_ed["win"], 5)
            junk = R[:, 0:QL]
            act.wait_ge(n_h, upto("m0", NT))
            act.wait_ge(n_hd, upto("m0", NT))
            for t in range(NT):
                link(act.activation(junk, lat[:, t, 0:QL], ACT.Square, accum_out=st[:, 80 + t:81 + t]))
                link(act.activation(junk[:, 0:KVL], lat[:, t, QL:QL + KVL], ACT.Square, accum_out=st[:, 85 + t:86 + t]))
            act.activation(st[:, 90:95], st[:, 80:85], ACT.Sqrt, scale=1.0 / QL, bias=const[:, C_EPS:C_EPS + 1]).then_inc(l_sd, 1)
            act.activation(st[:, 95:100], st[:, 85:90], ACT.Sqrt, scale=1.0 / KVL, bias=const[:, C_EPS:C_EPS + 1]).then_inc(l_sd, 1)
            for t in range(NT):
                act.wait_ge(l_tr, t + 1)
                act.activation(cqT[:, :, t * P:(t + 1) * P], bank(2 * (t % 2), QL).rearrange("p (c n) -> p c n", c=3), ACT.Copy).then_inc(l_ta, 1)
            act.wait_ge(k_rt, 1)
            link(act.activation(kTh[0][NOPE:QD, :], PS[0:ROPE, 0:768], ACT.Copy))
            act.activation(kTh[1][NOPE:QD, :], PS[0:ROPE, 0:768], ACT.Copy).then_inc(k_rc, 1)
            act.wait_ge(l_qr, 1)
            act.wait_ge(s_yz, 16 * (2 + XTILES - 1))
            act.wait_ge(m_cp, 6)
            for u in range(0, 20, 2):
                act.wait_ge(g_mm["uq"], u + 1)
                n, t = divmod(u, NT)
                act.activation(q[:, t, n * 384:(n + 1) * 384], bank(4, 384), ACT.Copy, scale=MLA_SCALE).then_inc(g_ea["uq"], 1)
            act.wait_ge(s_toepd, 16 * 16)
            for u in range(0, 24, 2):
                act.wait_ge(g_mm["uq"], 20 + u + 1)
                kt, n = divmod(u, 4)
                src = bank(4).rearrange("p (h c) -> p h c", h=4)
                act.activation(kn[:, kt, n * 256:(n + 1) * 256].rearrange("p (h c) -> p h c", h=4), src[:, :, 0:NOPE], ACT.Copy)
                act.activation(mv[:, kt, n * 256:(n + 1) * 256].rearrange("p (h c) -> p h c", h=4), src[:, :, NOPE:], ACT.Copy).then_inc(g_ea["uq"], 1)

            def o_out(l, s):
                h, t = divmod(s, NT)
                act.wait_ge(a_pv, tiles_(l, s + 1))
                act.wait_ge(a_ri, tiles_(l, s + 1))
                act.activation(O[:, t, h * VD:(h + 1) * VD], bank(6 + s % 2 * l, VD), ACT.Copy, scale=st[:, 108 + s % 4:109 + s % 4]).then_inc(a_o, 1)

            for i, u in enumerate(UNITS):
                b = 2 * (i % 2)
                h = u[1]
                act.wait_ge(a_u[0], i + 1)
                if u[0] == "K":
                    act.activation(kTh[h % 2][0:NOPE, :], PS[0:NOPE, b * 512:b * 512 + 768], ACT.Copy).then_inc(a_f[0], 1)
                elif u[0] == "Q":
                    act.activation(qTh[h % 2][0:QD, :], PS[0:QD, b * 512:b * 512 + 640], ACT.Copy).then_inc(a_f[0], 1)
                else:
                    s = h * NT + u[2]
                    n = 640 if u[2] < CTX else P
                    act.wait_ge(a_mx, tiles_(0, s + 1))
                    if s >= 2:
                        act.wait_ge(a_pt, tiles_(0, s - 1))
                    if s >= 4:
                        act.wait_ge(a_ri, tiles_(0, s - 3))
                    act.activation(Pm[s % 2][:, 0:n], bank(b, n), ACT.Exp, bias=st[:, 100 + s % 4:101 + s % 4],
                                   accum_out=st[:, 104 + s % 4:105 + s % 4]).then_inc(a_ex, 1)
                    act.wait_ge(a_ex, tiles_(0, s + 1))
                    act.nop().then_inc(a_f[0], 1)
                    if s >= 2:
                        o_out(0, s - 2)
            o_out(0, NS - 2)
            o_out(0, NS - 1)

            def oT_half(l):
                for c in range(0, KD, 2):
                    act.wait_ge(o_tr, KD * l + c + 1)
                    act.activation(OT[:, c, :], bank(0, 640), ACT.Copy).then_inc(o_ta, 1)

            def scores(l):
                act.wait_ge(rr_lg, NT * (l + 1))
                act.activation(rt[:, 0:80], bank(6, 80), ACT.Sigmoid).then_inc(rr_sg, 1)

            def moe(l):
                def rows_T(ready):
                    act.wait_ge(e_tr[l], ready)
                    act.activation(gatT[:, 0:4, :], bank(3).rearrange("p (c n) -> p c n", c=4), ACT.Copy).then_inc(e_ta[l], 1)

                def sigmoid(ready, free):
                    act.wait_ge(e_gu[l], ready)
                    if free is not None:
                        act.wait_ge(e_ga[l], free)
                    act.activation(sig, bank(0, DE), ACT.Sigmoid).then_inc(e_sg[l], 1)

                def y_out(ready, par, free, rows):
                    act.wait_ge(e_dn[l], ready)
                    act.wait_ge(e_ys[l][par], free)
                    act.activation(yb[par][:, 0:512], bank(1), ACT.Copy).then_inc(e_ya[l], 1)
                    act.wait_ge(e_ya[l], ready + 1)
                    act.wait_ge(e_yd[l], ready + 1)
                    act.dma_start(yD[rows, :], yb[par]).then_inc(e_ys[l][par], 16)

                act.nop().then_inc(e_ya[l], 1)
                for p in range(2):
                    act.nop().then_inc(e_ys[l][p], 16)
                rows_T(1)
                sigmoid(1, None)
                rows_T(2)
                act.wait_ge(rr_tab, l + 1)
                pairs = act.value_load(rtx[0:1, 31:32], min_val=8, max_val=12)
                with act.Fori(0, pairs) as i:
                    for j in range(2):
                        sigmoid(i * 2 + (2 + j), i * 2 + (1 + j))
                        rows_T(i * 2 + (3 + j))
                        y_out(i * 2 + (1 + j), j, i * 16 + 16, bass.ds(i * (2 * P) + j * P, P))
                y_out(pairs * 2 + 1, 0, pairs * 16 + 16, bass.ds(pairs * (2 * P), P))

            oT_half(0)
            norm("f0")
            scores(0)
            moe(0)

            norm("m1")
            act.wait_ge(kc_tr, 1)
            act.activation(kcT[:, 0:4, :], bank(0).rearrange("p (c n) -> p c n", c=4), ACT.Copy).then_inc(kc_ta, 1)
            for u in range(0, 16, 2):
                if u == 8:
                    act.wait_ge(m_cp, 24)
                act.wait_ge(qk_mm, u + 1)
                dst = qT[:, u, :] if u < 8 else kT[:, u - 8, :]
                act.activation(dst, bank(2, 640), ACT.Copy, scale=-NAT_SCALE if u < 8 else 1.0).then_inc(qk_ea, 1)

            def v_out(u):
                act.wait_ge(g_mm["vproj"], u + 1)
                j, t = divmod(u, NT)
                act.activation(nv[:, t, j * 512:(j + 1) * 512], bank(4), ACT.Copy).then_inc(g_ea["vproj"], 1)

            v_out(0)
            act.wait_ge(ko_tr, 1)
            act.activation(kout[:, 0:512], bank(0), ACT.Copy).then_inc(ko_ca, 1)
            for u in (2, 4, 6, 8):
                v_out(u)

            def queries(h):
                rows = slice(h % 2 * 64, h % 2 * 64 + 64)
                act.activation(qz[h % 2][rows, :], qT[rows, h // 2, :], ACT.Copy).then_inc(q_ok, 1)

            act.wait_ge(qk_ea, 4)
            act.wait_ge(qk_ed, 4)
            act.wait_ge(n_h, upto("m1", NT))
            queries(0)
            queries(1)
            for s in range(NS + 3):
                if s < NS:
                    t = s % NT
                    act.wait_ge(a_mx, tiles_(1, s + 1))
                    if s >= 4:
                        act.wait_ge(a_ri, tiles_(1, s - 3))
                    if t < CTX:
                        src, n = Pn[s % 2], 384
                    else:
                        src, n = bank(s % 4, P), P
                        if s >= 2:
                            act.wait_ge(a_pt, tiles_(1, s - 1))
                    act.activation(Pn[s % 2][:, 0:n], src, ACT.Exp, scale=-1.0, bias=st[:, 100 + s % 4:101 + s % 4],
                                   accum_out=st[:, 104 + s % 4:105 + s % 4]).then_inc(a_ex, 1)
                if s >= 3:
                    o_out(1, s - 3)
                if s < NS and s % NT == 2 and NT <= s < (H - 1) * NT:
                    act.wait_ge(a_u[1], s // NT * NT)
                    queries(s // NT + 1)
            oT_half(1)
            norm("f1")
            scores(1)
            moe(1)
            norm("fin")

        @block.vector
        def _(dve):
            chain = [0]

            def link(ins):
                chain[0] += 1
                ins.then_inc(s_dve, 1)
                dve.wait_ge(s_dve, chain[0])

            def tt(dst, x, y, op):
                return dve.tensor_tensor(dst, x, y, op)

            def norm(s, x_tile=None):
                i = NORMS.index(s)
                sd, rs = (st[:, n + 5 * i:n + 5 * i + 5] for n in (25, 50))
                lag = NT if s[0] == "f" and s != "fin" else 2
                if x_tile:
                    x_tile(0)
                for t in range(NT + lag):
                    if t < NT:
                        if x_tile and t + 1 < NT:
                            x_tile(t + 1)
                        dve.wait_ge(n_sd, upto(s, t + 1))
                        dve.reciprocal(rs[:, t:t + 1], sd[:, t:t + 1]).then_inc(n_rs, 1)
                        if t == 0:
                            dve.wait_ge(r_ab, 64 * (i + 1) if s != "fin" else 64 * 4 + 16)
                        dve.wait_ge(n_rs, upto(s, t + 1))
                        dve.scalar_tensor_tensor(out=HB[t], in0=x_(t), scalar=rs[:, t:t + 1], in1=row(t // CTX if s != "fin" else 0),
                                                 op0=ALU.mult, op1=ALU.mult).then_inc(n_ha, 1)
                        if s != "fin":
                            dve.wait_ge(n_ha, upto(s, t + 1))
                            tt(HB[t][:, NH:], HB[t][:, NH:], row(2 + t // CTX)[:, NH:], ALU.add).then_inc(n_hd, 1)
                    if s == "f0" and t >= lag:
                        ada_rows(12 + t - lag)
                    if t >= lag and s != "fin":
                        v = t - lag
                        dve.wait_ge(n_tr, upto(s, v + 1))
                        dve.tensor_copy(hT[:, 4:8, v * P:(v + 1) * P],
                                        bank(2 * (v % 2) + 1).rearrange("p (c n) -> p c n", c=4)).then_inc(n_td, 1)

            def ada_rows(i):
                dve.wait_ge(m_mm, i + 1)
                dve.wait_ge(m_b, 16 * (i + 1))
                if i >= 1:
                    dve.wait_ge(m_st, 16 * i)
                bias = ada_bias(i)
                ins = tt(modrow, PS[0:2, ada_bank(i) * 512:ada_bank(i) * 512 + 512], bias[:, 0:512], ALU.add)
                if i % 12 in (2, 3, 8, 9):
                    link(ins)
                    ins = dve.scalar_tensor_tensor(out=modrow, in0=modrow, scalar=1.0, in1=bias[:, 512:1024], op0=ALU.add, op1=ALU.mult)
                ins.then_inc(m_cp, 1)

            dve.wait_ge(s_vt, 1)
            dve.tensor_copy(vecT[:, :], bank(6, 16)).then_inc(s_vc, 1)
            dve.wait_ge(s_vc, 1)
            dve.wait_ge(s_sg, 1)
            tt(condT[:, :].rearrange("p (k c) -> p c k", c=2), vecT[:, :].rearrange("p (c k) -> p c k", c=2),
               st[:, 144:160].rearrange("p (c k) -> p c k", c=2), ALU.mult).then_inc(s_cond, 1)
            dve.wait_ge(s_rpb, 16)
            link(dve.memset(toep, -NEG))
            for v, (d0, d1) in enumerate(((0, 31), (7, 23))):
                for r in range(ROWS):
                    ins = dve.tensor_scalar(toep[:, v, r, 16 + d0:16 + d1, :], rpbs[:, d0:d1, 7 - r:15 - r], -1.0, None, ALU.mult)
            ins.then_inc(s_toep, 1)
            for i in range(4):
                ada_rows(i)
            norm("m0")

            for u in range(1, 10, 2):
                dve.wait_ge(g_mm["win"], u + 1)
                dve.tensor_copy(lat[:, u % NT, u // NT * 336:(u // NT + 1) * 336], bank(5, 336)).then_inc(g_ed["win"], 1)
            dve.wait_ge(l_sd, 2)
            dve.reciprocal(st[:, 90:100], st[:, 90:100]).then_inc(l_rs, 1)
            dve.wait_ge(l_rs, 1)
            dve.wait_ge(s_par, 64)
            dve.wait_ge(g_ea["win"], 5)
            for t in range(NT):
                for (c0, c1), i in (((0, QL), 90), ((QL, QL + KVL), 95)):
                    dve.scalar_tensor_tensor(out=lat[:, t, c0:c1], in0=lat[:, t, c0:c1], scalar=st[:, i + t:i + t + 1],
                                             in1=latG[:, c0:c1], op0=ALU.mult, op1=ALU.mult).then_inc(l_n, 1)
            ada_rows(4)
            ada_rows(5)
            for t in range(6):
                dve.wait_ge(l_tr, t + 1)
                kt = (0, 1, 2, 3, 5, 4)[t]
                dve.tensor_copy(ckvT[:, :, kt * P:(kt + 1) * P], bank(2 * (t % 2) + 1, KVL).rearrange("p (c n) -> p c n", c=2)).then_inc(l_td, 1)
            dve.wait_ge(s_yz, 16 * (2 + XTILES - 1))
            dve.wait_ge(l_qr, 1)
            for u in range(1, 20, 2):
                dve.wait_ge(g_mm["uq"], u + 1)
                n, t = divmod(u, NT)
                dve.tensor_scalar(q[:, t, n * 384:(n + 1) * 384], bank(5, 384), MLA_SCALE, None, ALU.mult).then_inc(g_ed["uq"], 1)
            dve.wait_ge(s_toepd, 16 * 16)
            for u in range(1, 24, 2):
                dve.wait_ge(g_mm["uq"], 20 + u + 1)
                kt, n = divmod(u, 4)
                src = bank(5).rearrange("p (h c) -> p h c", h=4)
                dve.tensor_copy(kn[:, kt, n * 256:(n + 1) * 256].rearrange("p (h c) -> p h c", h=4), src[:, :, 0:NOPE])
                dve.tensor_copy(mv[:, kt, n * 256:(n + 1) * 256].rearrange("p (h c) -> p h c", h=4), src[:, :, NOPE:]).then_inc(g_ed["uq"], 1)

            def rinv(l, s):
                dve.wait_ge(a_ex, tiles_(l, s + 1))
                if s >= 4:
                    dve.wait_ge(a_o, tiles_(l, s - 3))
                dve.reciprocal(st[:, 108 + s % 4:109 + s % 4], st[:, 104 + s % 4:105 + s % 4]).then_inc(a_ri, 1)

            def pT_out(l, s, dst, src, n):
                dve.wait_ge(a_pt, tiles_(l, s + 1))
                if s >= 2:
                    dve.wait_ge(a_pv, tiles_(l, s - 1))
                dve.tensor_copy(dst[:, 0:n], src).then_inc(a_pe, 1)

            for s in range(NS + 1):
                if s < NS:
                    i = AT["S", s // NT, s % NT]
                    n = 640 if s % NT < CTX else P
                    dve.wait_ge(a_u[0], i + 1)
                    if s >= 4:
                        dve.wait_ge(a_ex, tiles_(0, s - 3))
                    dve.tensor_reduce(st[:, 100 + s % 4:101 + s % 4], bank(2 * (i % 2), n), AXX, ALU.max, negate=True).then_inc(a_mx, 1)
                if s >= 1:
                    n = 640 if (s - 1) % NT < CTX else P
                    rinv(0, s - 1)
                    pT_out(0, s - 1, PTm[(s - 1) % 2], bank(4, n), n)
                if s % NT == CTX and s < 6 * NT:
                    ada_rows(6 + s // NT)

            def out_projection(l):
                for c in range(1, KD, 2):
                    dve.wait_ge(o_tr, KD * l + c + 1)
                    dve.tensor_copy(OT[:, c, :], bank(2, 640)).then_inc(o_td, 1)
                name = f"wo{l}"
                dve.wait_ge(r_g, 32 * (2 * l + 1))

                def x_tile(t):
                    for j in range(2):
                        u = 2 * t + j
                        dve.wait_ge(g_mm[name], u + 1)
                        tt(tmpw[j], bank(4 + j), row(4 + t // CTX)[:, j * 512:(j + 1) * 512], ALU.mult).then_inc(g_ed[name], 1)
                        dve.wait_ge(g_ed[name], u + 1)
                        xs = x_(t)[:, j * 512:(j + 1) * 512]
                        ins = tt(xs, xs, tmpw[j], ALU.add)
                        if j == 1:
                            ins.then_inc(x_rdy, 1)

                norm(f"f{l}", x_tile)

            def routing(l):
                def v3(at, n=80, t=NT):
                    return rt[:, at:at + n].rearrange("p (t e) -> p t e", t=t)

                sc, bi, ms, ky, tm = (v3(c) for c in (0, 80, 160, 240, 560))
                oh = [v3(320), v3(400)]
                M, pos = v3(MZ + E), v3(640)
                gg = [rt[:, 720 + 20 * i:740 + 20 * i].rearrange("p (t g) -> p t g", t=NT) for i in range(10)]
                sm = [rt[:, 920 + 5 * i:925 + 5 * i] for i in range(12)]
                cs, ext, pf, pg, base = (rt[:, 1000 + 16 * i:1016 + 16 * i] for i in range(5))
                tx, cmp_, pay = rt[0:1, 1100:1132], rt[0:1, 1140:1284], rt[:, 1290:1310]

                def over(v, n):
                    return v.unsqueeze(2).to_broadcast([P, NT, n])

                def iota(at, n):
                    return const[:, at:at + n].unsqueeze(1).to_broadcast([P, NT, n])

                def reduce(dst, src, op):
                    link(dve.tensor_reduce(dst, src, AXX, op))

                def first_max(dst, v, n, mx, kmin, key):
                    reduce(mx, v, ALU.max)
                    link(tt(key, v, over(mx, n), ALU.is_equal))
                    link(dve.scalar_tensor_tensor(out=key, in0=key, scalar=-64.0, in1=iota(C_I16, n), op0=ALU.mult, op1=ALU.add))
                    reduce(kmin, key, ALU.min)
                    link(tt(dst, key, over(kmin, n), ALU.is_equal))

                dve.wait_ge(rr_sg, l + 1)
                dve.wait_ge(s_par, 64)
                link(tt(bi, sc, rt[:, 1320:1336].unsqueeze(1).to_broadcast([P, NT, E]), ALU.add))
                b4 = rt[:, 80:160].rearrange("p (t g j) -> p t g j", t=NT, g=G4)
                b = [b4[:, :, :, j] for j in range(4)]
                link(tt(gg[0], b[0], b[1], ALU.max))
                link(tt(gg[1], b[0], b[1], ALU.min))
                link(tt(gg[2], b[2], b[3], ALU.max))
                link(tt(gg[3], b[2], b[3], ALU.min))
                link(tt(gg[4], gg[0], gg[2], ALU.max))
                link(tt(gg[5], gg[0], gg[2], ALU.min))
                link(tt(gg[6], gg[1], gg[3], ALU.max))
                link(tt(gg[5], gg[5], gg[6], ALU.max))
                link(tt(gg[4], gg[4], gg[5], ALU.add))
                first_max(gg[8], gg[4], G4, sm[0], sm[1], gg[7])
                gm = rt[:, 880:900].rearrange("p (t g) -> p t g", t=NT).unsqueeze(3).to_broadcast([P, NT, G4, 4])
                m4 = rt[:, 160:240].rearrange("p (t g j) -> p t g j", t=NT, g=G4)
                link(tt(m4, b4, gm, ALU.mult))
                link(dve.tensor_scalar(gg[9], gg[8], 1.0, -NEG, ALU.subtract, ALU.mult))
                g9 = rt[:, 900:920].rearrange("p (t g) -> p t g", t=NT).unsqueeze(3).to_broadcast([P, NT, G4, 4])
                link(tt(m4, m4, g9, ALU.add))
                for c in range(2):
                    first_max(oh[c], ms, E, sm[2], sm[3], ky)
                    if c == 0:
                        link(dve.scalar_tensor_tensor(out=ms, in0=oh[0], scalar=3 * NEG, in1=ms, op0=ALU.mult, op1=ALU.add))
                link(dve.memset(rt[:, MZ:MZ + E], 0.0))
                tt(M, oh[0], oh[1], ALU.add).then_inc(rr_m, 1)
                for c in range(2):
                    link(tt(tm, oh[c], sc, ALU.mult))
                    reduce(sm[4 + c], tm, ALU.add)
                link(tt(sm[6], sm[4], sm[5], ALU.add))
                link(dve.reciprocal(sm[7], sm[6]))
                p4 = pay.rearrange("p (t c w) -> p t c w", t=NT, c=2)
                pu = rt[:, 1290:1310].bitcast(U32).rearrange("p (t c w) -> p t c w", t=NT, c=2)
                for c in range(2):
                    link(tt(p4[:, :, c, 1], sm[4 + c], sm[7], ALU.mult))
                    link(dve.tensor_copy(pu[:, :, c, 0], const[:, C_TOK:C_TOK + NT]))
                if l == 0:
                    ada_rows(12 + NT)
                    ada_rows(13 + NT)
                dve.wait_ge(rr_cnt, l + 1)
                link(dve.tensor_copy(cs, bank(7, E, NT * E)))
                link(dve.tensor_copy(tm, bank(7, 80).rearrange("p (t e) -> p t e", t=NT)))
                link(dve.tensor_scalar(ext, cs, float(P), None, ALU.is_gt))
                for j in range(2, NT):
                    link(dve.scalar_tensor_tensor(out=ext, in0=cs, scalar=float(P * j), in1=ext, op0=ALU.is_gt, op1=ALU.add))
                src, dst = ext, pf
                for n in (1, 2, 4, 8):
                    link(dve.tensor_copy(dst[:, 0:n], src[:, 0:n]))
                    link(tt(dst[:, n:E], src[:, n:E], src[:, 0:E - n], ALU.add))
                    src, dst = dst, (pg if dst is pf else pf)
                incl = src
                link(tt(base, incl, ext, ALU.subtract))
                link(dve.tensor_scalar(base, base, float(P), float(P * (E - 1)), ALU.mult, ALU.add))
                e128 = const[:, C_E128:C_E128 + E]
                link(tt(base, base, e128, ALU.subtract))
                link(dve.tensor_scalar(ky, tm, float(P), None, ALU.is_ge))
                link(tt(ky, ky, base.unsqueeze(1).to_broadcast([P, NT, E]), ALU.mult))
                link(tt(ky, ky, tm, ALU.add))
                link(tt(pos, ky, iota(C_E128, E), ALU.add))
                ru = rti[:, :].rearrange("p (t c) -> p t c", c=2)
                for c in range(2):
                    link(tt(tm, oh[c], pos, ALU.mult))
                    reduce(sm[8 + c], tm, ALU.add)
                    link(dve.tensor_copy(ru[:, :, c], sm[8 + c]))
                dve.nop().then_inc(rr_pos, 1)
                link(dve.memset(tx, 0.0))
                link(dve.tensor_copy(tx[:, 0:E], const[0:1, C_I16:C_I16 + E]))
                cm = cmp_.rearrange("p (x e) -> p x e", x=XTILES)
                link(tt(cm, incl[0:1, :].unsqueeze(1).to_broadcast([1, XTILES, E]),
                        const[0:1, C_X9:C_X9 + XTILES].unsqueeze(2).to_broadcast([1, XTILES, E]), ALU.is_le))
                reduce(tx[:, E:MAXT], cm, ALU.add)
                link(dve.tensor_scalar(tx[:, E:MAXT], tx[:, E:MAXT], float(E - 1), None, ALU.min))
                link(dve.tensor_scalar(cmp_[:, 0:4], const[0:1, C_EVEN:C_EVEN + 4], incl[0:1, E - 1:E], None, ALU.is_le))
                reduce(cmp_[:, 4:5], cmp_[:, 0:4], ALU.add)
                link(dve.tensor_scalar(tx[:, 31:32], cmp_[:, 4:5], 8.0, None, ALU.add))
                dve.tensor_copy(rtx[:, :], tx).then_inc(rr_tab, 1)

            def moe(l):
                def rows_T(ready):
                    dve.wait_ge(e_tr[l], ready)
                    dve.tensor_copy(gatT[:, 4:8, :], bank(4).rearrange("p (c n) -> p c n", c=4)).then_inc(e_td[l], 1)

                def acts(par, ready, free, gates):
                    dve.wait_ge(e_gt[l][par], gates)
                    dve.wait_ge(e_sg[l], ready)
                    tt(sig, sig, bank(0, DE), ALU.mult).then_inc(e_ga[l], 1)
                    dve.wait_ge(e_ga[l], ready)
                    if free is not None:
                        dve.wait_ge(e_at[l], free)
                    dve.scalar_tensor_tensor(out=actv, in0=sig, scalar=info[:, 5 + 2 * par:6 + 2 * par], in1=bank(0, DE, DE),
                                             op0=ALU.mult, op1=ALU.mult).then_inc(e_ac[l], 1)

                def acts_T(ready):
                    dve.wait_ge(e_at[l], ready)
                    dve.tensor_copy(actT, bank(5, DE).rearrange("p (c n) -> p c n", c=2)).then_inc(e_ae[l], 1)

                def y_out(ready, par, free):
                    dve.wait_ge(e_dn[l], ready)
                    dve.wait_ge(e_ys[l][par], free)
                    dve.tensor_copy(yb[par][:, 512:], bank(2)).then_inc(e_yd[l], 1)

                dve.nop().then_inc(e_yd[l], 1)
                rows_T(1)
                acts(0, 1, None, 16)
                rows_T(2)
                acts_T(1)
                pairs = dve.value_load(rtx[0:1, 31:32], min_val=8, max_val=12)
                with dve.Fori(0, pairs) as i:
                    for j in range(2):
                        acts(1 - j, i * 2 + (2 + j), i * 2 + (1 + j), i * 16 + 16 * (1 + j))
                        rows_T(i * 2 + (3 + j))
                        y_out(i * 2 + (1 + j), j, i * 16 + 16)
                        acts_T(i * 2 + (2 + j))
                y_out(pairs * 2 + 1, 0, pairs * 16 + 16)

            def combine(l, nxt):
                dve.wait_ge(r_g, 32 * (2 * l + 2))

                def x_tile(t):
                    y0, y1 = cy[t]
                    if t < 2:
                        dve.wait_ge(c_in[t], 32 * (l + 1))
                        link(tt(y0, y0, y1, ALU.add))
                    else:
                        dve.wait_ge(c_sum, (NT - 2) * l + t - 1)
                    link(tt(y0, y0, row(4 + t // CTX), ALU.mult))
                    tt(x_(t), x_(t), y0, ALU.add).then_inc(x_rdy, 1)

                norm(nxt, x_tile)

            out_projection(0)
            routing(0)
            for i in range(14 + NT, 12 + GAP_ADA):
                ada_rows(i)
            moe(0)
            ada_rows(23)
            combine(0, "m1")

            dve.wait_ge(kc_tr, 1)
            dve.tensor_copy(kcT[:, 4:8, :], bank(1).rearrange("p (c n) -> p c n", c=4)).then_inc(kc_td, 1)
            for u in range(1, 16, 2):
                dve.wait_ge(qk_mm, u + 1)
                if u < 8:
                    dve.tensor_scalar(qT[:, u, :], bank(0, 640), -NAT_SCALE, None, ALU.mult).then_inc(qk_ed, 1)
                else:
                    dve.tensor_copy(kT[:, u - 8, :], bank(0, 640)).then_inc(qk_ed, 1)

            def v_out(u):
                dve.wait_ge(g_mm["vproj"], u + 1)
                j, t = divmod(u, NT)
                dve.tensor_copy(nv[:, t, j * 512:(j + 1) * 512], bank(5)).then_inc(g_ed["vproj"], 1)

            v_out(1)
            dve.wait_ge(ko_tr, 1)
            dve.tensor_copy(kout[:, 512:], bank(1)).then_inc(ko_cd, 1)
            for u in (3, 5, 7, 9):
                v_out(u)
            for s in range(NS + 2):
                if s < NS:
                    h, t = divmod(s, NT)
                    dve.wait_ge(a_u[1], s + 1)
                    if s >= 4:
                        dve.wait_ge(a_ex, tiles_(1, s - 3))
                    neg = st[:, 100 + s % 4:101 + s % 4]
                    if t < CTX:
                        if s >= 2:
                            dve.wait_ge(a_pt, tiles_(1, s - 1))
                        if t == 0:
                            dve.wait_ge(b_in[h % 2], 48 * (h // 2 + 1))
                            dve.wait_ge(b_ok, 2 * (h + 1))
                        dve.tensor_tensor_reduce(out=Pn[s % 2], in0=bank(s % 4, 384), in1=biasb[h % 2][:, VARIANT[t], :], scale=1.0,
                                                 scalar=-3 * NEG, op0=ALU.add, op1=ALU.min, accum_out=neg).then_inc(a_mx, 1)
                    else:
                        dve.tensor_reduce(neg, bank(s % 4, P), AXX, ALU.min).then_inc(a_mx, 1)
                if s >= 1 and s - 1 < NS:
                    rinv(1, s - 1)
                if s >= 2:
                    n = 384 if (s - 2) % NT < CTX else P
                    pT_out(1, s - 2, PTn[s % 2], bank(4 + s % 2, n), n)
            out_projection(1)
            routing(1)
            moe(1)
            combine(1, "fin")


def kernel(**inputs):
    import concourse.bacc as bacc
    from concourse.bass_utils import run_bass_kernel_spmd as run

    a = {n: np.asarray(v) for n, v in inputs.items()}

    def chunks(w, cols):
        k, n = w.shape
        v = w.reshape(k // P, P, n // cols, cols).transpose(2, 1, 0, 3)
        return np.ascontiguousarray(v).reshape(n // cols, P, -1)

    x = a["x_sample"][0].reshape(ROWS, GRID_W, D).transpose(1, 0, 2).reshape(-1, D)
    gu = np.stack([a["moe_w_gate"], a["moe_w_up"]], 3)
    gu = gu.reshape(DEPTH, E, KD, P, 2 * DE).transpose(0, 1, 3, 2, 4)
    down = a["moe_w_down"].reshape(DEPTH, E, 2, P, D).transpose(0, 1, 3, 2, 4)
    adab = np.zeros((DEPTH, 12, 2, 1024), np.float32)
    adab[:, :, :, 0:512] = a["b_ada"].reshape(DEPTH, 12, 1, 512)
    adab[:, 2:4, :, 512:] = a["norm_mix"].reshape(DEPTH, 2, 1, 512)
    adab[:, 8:10, :, 512:] = a["norm_ffn"].reshape(DEPTH, 2, 1, 512)
    arrays = {
        "const": constants(),
        "x": np.concatenate([x, a["x_prompt"][0]], 0),
        "cond": np.concatenate([a["c"].reshape(8, P), a["c_ctx"].reshape(8, P)], 0),
        "adab": adab,
        "ada": np.stack([chunks(w, 512) for w in a["w_ada"]], 0),
        "win": chunks(a["mla_w_in"][0], 336),
        "uq": chunks(a["mla_w_uq"][0], 768),
        "ukv": chunks(a["mla_w_ukv"][0], 2048)[0],
        "wo0": chunks(a["mla_w_o"][0], 512),
        "qkv": chunks(a["nat_w_qkv"][0], 512),
        "wo1": chunks(a["nat_w_o"][0], 512),
        "gu": gu.reshape(DEPTH, E, P, KD * 2 * DE),
        "down": down.reshape(DEPTH, E, P, 2 * D),
        "wr": a["w_router"].reshape(KD, P, E).transpose(1, 0, 2).reshape(P, KD * E),
        "rbias": a["router_bias"].reshape(1, E),
        "rpb": a["nat_rpb"][0].transpose(0, 2, 1).reshape(H, -1),
        "qnorm": a["mla_q_norm"].reshape(1, QL),
        "kvnorm": a["mla_kv_norm"].reshape(1, KVL),
        "gfin": a["norm_final"].reshape(1, D),
        "ckv": a["cache_mla_ckv"][0, 0],
        "krope": a["cache_mla_krope"][0, 0],
        "natk": a["cache_nat_k"][0, 0].reshape(P, D),
        "natv": a["cache_nat_v"][0, 0].reshape(P, D),
    }
    nc = bacc.Bacc("TRN2", target_bir_lowering=False, num_devices=1)
    arrays = {f"in_{n}": np.ascontiguousarray(v) for n, v in arrays.items()}
    ins = {n[3:]: nc.dram_tensor(n, v.shape, F32, kind="ExternalInput").ap() for n, v in arrays.items()}
    outs = {n: nc.dram_tensor(f"out_{n}", s, F32, kind="ExternalOutput").ap() for n, s in (
        ("y", (TOK, D)), ("ckv", (P, KVL)), ("krope", (P, ROPE)), ("k", (P, D)), ("v", (P, D)))}
    build(nc, ins, outs)
    r = run(nc, [arrays], core_ids=[0]).results[0]
    y = r["out_y"]
    ys = y[:512].reshape(GRID_W, ROWS, D).transpose(1, 0, 2).reshape(1, 512, D)
    return (y[512:].reshape(1, P, D), ys, r["out_ckv"].reshape(1, 1, P, KVL), r["out_krope"].reshape(1, 1, P, ROPE),
            r["out_k"].reshape(1, 1, P, H, 64), r["out_v"].reshape(1, 1, P, H, 64))
```
